# Optimizing a Trainium2 kernel written in Bass

```python
import jax, jax.numpy as jnp
from jax import lax
import numpy as np

D_MODEL = 1024
BATCH = 1
SEQ = 256
DEPTH = 2

N_MIXERS = 2
N_HEADS = 16
N_KV_HEADS = 4
HEAD_DIM = D_MODEL // N_HEADS
GROUP = N_HEADS // N_KV_HEADS
QKV_DIM = (N_HEADS + 2 * N_KV_HEADS) * HEAD_DIM
WINDOW = 128
BLOCK = 128
ROPE_THETA = 10000.0
CONV_WIDTH = 31
CONV_HALF = CONV_WIDTH // 2
D_FF = 3584
N_EXPERTS = 8
TOP_K = 2
LN_EPS = 1e-5
N_EVEN = (DEPTH + 1) // 2
N_ODD = DEPTH // 2
DN_ALPHA = (2 * DEPTH) ** 0.25
DN_BETA = (8 * DEPTH) ** -0.25
NEG_INF = -1e30

kernel_name = 'hybrid_swa_conformer_moe_deepnorm'

def layer_norm(x, g, b):
    xf = x.astype(jnp.float32)
    mu = jnp.mean(xf, axis=-1, keepdims=True)
    var = jnp.mean(jnp.square(xf - mu), axis=-1, keepdims=True)
    y = (xf - mu) * lax.rsqrt(var + LN_EPS) * g.astype(jnp.float32) + b.astype(jnp.float32)
    return y.astype(x.dtype)

def rope(t, cos, sin):
    tf = t.astype(jnp.float32)
    t1, t2 = jnp.split(tf, 2, axis=-1)
    rot = jnp.concatenate([-t2, t1], axis=-1)
    return (tf * cos[None, :, None, :] + rot * sin[None, :, None, :]).astype(t.dtype)

def windowed_gqa(x, w_qkv, sink, w_o):
    B, S, _ = x.shape
    nb = S // BLOCK
    qkv = x @ w_qkv
    q, k, v = jnp.split(qkv, [N_HEADS * HEAD_DIM, (N_HEADS + N_KV_HEADS) * HEAD_DIM], axis=-1)
    q = q.reshape(B, S, N_HEADS, HEAD_DIM)
    k = k.reshape(B, S, N_KV_HEADS, HEAD_DIM)
    v = v.reshape(B, S, N_KV_HEADS, HEAD_DIM)
    pos = jnp.arange(S, dtype=jnp.float32)
    inv_freq = ROPE_THETA ** (-jnp.arange(0, HEAD_DIM, 2, dtype=jnp.float32) / HEAD_DIM)
    ang = pos[:, None] * inv_freq[None, :]
    ang = jnp.concatenate([ang, ang], axis=-1)
    cos, sin = jnp.cos(ang), jnp.sin(ang)
    q = rope(q, cos, sin).reshape(B, nb, BLOCK, N_KV_HEADS, GROUP, HEAD_DIM)
    k = rope(k, cos, sin)

    def band(t):
        tp = jnp.pad(t, ((0, 0), (BLOCK, BLOCK), (0, 0), (0, 0)))
        tp = tp.reshape(B, nb + 2, BLOCK, N_KV_HEADS, HEAD_DIM)
        return jnp.concatenate([tp[:, :-2], tp[:, 1:-1], tp[:, 2:]], axis=2)

    kb, vb = band(k), band(v)
    s = jnp.einsum('bnqkgd,bnjkd->bnkgqj', q, kb).astype(jnp.float32) * (HEAD_DIM ** -0.5)
    blk = jnp.arange(nb)[:, None, None] * BLOCK
    qpos = blk + jnp.arange(BLOCK)[None, :, None]
    kpos = blk - BLOCK + jnp.arange(3 * BLOCK)[None, None, :]
    valid = (jnp.abs(kpos - qpos) <= WINDOW) & (kpos >= 0) & (kpos < S)
    s = jnp.where(valid[None, :, None, None], s, NEG_INF)
    sk = sink.astype(jnp.float32).reshape(N_KV_HEADS, GROUP)[None, None, :, :, None, None]
    m = jnp.maximum(jnp.max(s, axis=-1, keepdims=True), sk)
    p = jnp.exp(s - m)
    p = p / (jnp.sum(p, axis=-1, keepdims=True) + jnp.exp(sk - m))
    o = jnp.einsum('bnkgqj,bnjkd->bnqkgd', p.astype(vb.dtype), vb)
    return o.reshape(B, S, N_HEADS * HEAD_DIM) @ w_o

def conformer_conv(x, pw1_w, pw1_b, dw_w, dw_b, norm_g, norm_b, pw2_w, pw2_b):
    h = x @ pw1_w + pw1_b
    a, g = jnp.split(h, 2, axis=-1)
    h = a * jax.nn.sigmoid(g)
    h = lax.conv_general_dilated(
        h, dw_w[:, None, :].astype(h.dtype), window_strides=(1,),
        padding=[(CONV_HALF, CONV_HALF)],
        dimension_numbers=('NWC', 'WIO', 'NWC'),
        feature_group_count=D_MODEL) + dw_b
    h = jax.nn.silu(layer_norm(h, norm_g, norm_b))
    return h @ pw2_w + pw2_b

def swiglu(x, w_gate, w_up, w_down):
    return (jax.nn.silu(x @ w_gate) * (x @ w_up)) @ w_down

def moe_swiglu(x, router, w_gate, w_up, w_down):
    B, S, D = x.shape
    xt = x.reshape(B * S, D)
    logits = (xt @ router).astype(jnp.float32)
    top_v, top_i = lax.top_k(logits, TOP_K)
    gates = jax.nn.softmax(top_v, axis=-1)
    combine = jnp.sum(jax.nn.one_hot(top_i, N_EXPERTS, dtype=jnp.float32) * gates[..., None], axis=1)
    y = jnp.zeros((B * S, D), jnp.float32)
    for e in range(N_EXPERTS):
        y = y + combine[:, e:e + 1] * swiglu(xt, w_gate[e], w_up[e], w_down[e]).astype(jnp.float32)
    return y.astype(x.dtype).reshape(B, S, D)

def setup_inputs(seed: int = 0) -> dict:
    key = jax.random.key(seed)
    ks = jax.random.split(key, 24)
    f32 = jnp.float32

    def nrm(k, shape, scale):
        return jax.random.normal(k, shape, f32) * scale

    d_in = D_MODEL ** -0.5
    w_qk = nrm(ks[1], (N_EVEN, D_MODEL, (N_HEADS + N_KV_HEADS) * HEAD_DIM), d_in)
    w_v = nrm(ks[2], (N_EVEN, D_MODEL, N_KV_HEADS * HEAD_DIM), d_in * DN_BETA)
    return {
        'x': jax.random.normal(ks[0], (BATCH, SEQ, D_MODEL), f32),
        'attn_w_qkv': jnp.concatenate([w_qk, w_v], axis=-1),
        'attn_sink': nrm(ks[3], (N_EVEN, N_HEADS), 0.5),
        'attn_w_o': nrm(ks[4], (N_EVEN, N_HEADS * HEAD_DIM, D_MODEL), d_in * DN_BETA),
        'conv_pw1_w': nrm(ks[5], (N_ODD, D_MODEL, 2 * D_MODEL), d_in),
        'conv_pw1_b': nrm(ks[6], (N_ODD, 2 * D_MODEL), 0.02),
        'conv_dw_w': nrm(ks[7], (N_ODD, CONV_WIDTH, D_MODEL), CONV_WIDTH ** -0.5),
        'conv_dw_b': nrm(ks[8], (N_ODD, D_MODEL), 0.02),
        'conv_norm_g': 1.0 + nrm(ks[9], (N_ODD, D_MODEL), 0.02),
        'conv_norm_b': nrm(ks[10], (N_ODD, D_MODEL), 0.02),
        'conv_pw2_w': nrm(ks[11], (N_ODD, D_MODEL, D_MODEL), d_in * DN_BETA),
        'conv_pw2_b': nrm(ks[12], (N_ODD, D_MODEL), 0.02),
        'ffn_w_gate': nrm(ks[13], (N_EVEN, D_MODEL, D_FF), d_in),
        'ffn_w_up': nrm(ks[14], (N_EVEN, D_MODEL, D_FF), d_in),
        'ffn_w_down': nrm(ks[15], (N_EVEN, D_FF, D_MODEL), D_FF ** -0.5 * DN_BETA),
        'moe_router': nrm(ks[16], (N_ODD, D_MODEL, N_EXPERTS), d_in),
        'moe_w_gate': nrm(ks[17], (N_ODD, N_EXPERTS, D_MODEL, D_FF), d_in),
        'moe_w_up': nrm(ks[18], (N_ODD, N_EXPERTS, D_MODEL, D_FF), d_in),
        'moe_w_down': nrm(ks[19], (N_ODD, N_EXPERTS, D_FF, D_MODEL), D_FF ** -0.5 * DN_BETA),
        'ln_mix_g': 1.0 + nrm(ks[20], (DEPTH, D_MODEL), 0.02),
        'ln_mix_b': nrm(ks[21], (DEPTH, D_MODEL), 0.02),
        'ln_ffn_g': 1.0 + nrm(ks[22], (DEPTH, D_MODEL), 0.02),
        'ln_ffn_b': nrm(ks[23], (DEPTH, D_MODEL), 0.02),
    }

def reference(x, attn_w_qkv, attn_sink, attn_w_o, conv_pw1_w, conv_pw1_b, conv_dw_w, conv_dw_b,
              conv_norm_g, conv_norm_b, conv_pw2_w, conv_pw2_b, ffn_w_gate, ffn_w_up, ffn_w_down,
              moe_router, moe_w_gate, moe_w_up, moe_w_down, ln_mix_g, ln_mix_b, ln_ffn_g, ln_ffn_b):
    for i in range(DEPTH):
        j = i // N_MIXERS
        if i % N_MIXERS == 0:
            mix = windowed_gqa(x, attn_w_qkv[j], attn_sink[j], attn_w_o[j])
        else:
            mix = conformer_conv(x, conv_pw1_w[j], conv_pw1_b[j], conv_dw_w[j], conv_dw_b[j],
                                 conv_norm_g[j], conv_norm_b[j], conv_pw2_w[j], conv_pw2_b[j])
        x = layer_norm(DN_ALPHA * x + mix, ln_mix_g[i], ln_mix_b[i])
        if i % 2 == 0:
            ffn = swiglu(x, ffn_w_gate[j], ffn_w_up[j], ffn_w_down[j])
        else:
            ffn = moe_swiglu(x, moe_router[j], moe_w_gate[j], moe_w_up[j], moe_w_down[j])
        x = layer_norm(DN_ALPHA * x + ffn, ln_ffn_g[i], ln_ffn_b[i])
    return x


_drawn_inputs = setup_inputs


def setup_inputs(seed=0):
    import zlib

    import numpy as np

    out = dict(_drawn_inputs(seed))
    spreads = {}
    factors = {'attn_sink': 34.743,
     'conv_pw1_b': 8.0,
     'conv_dw_b': 6.663,
     'conv_norm_g': 8.0,
     'conv_norm_b': 22.55,
     'conv_pw2_b': 2.709}
    for name, (base, spread) in spreads.items():
        noise = np.random.default_rng([zlib.crc32(name.encode()), seed]).standard_normal(out[name].shape)
        drawn = base * np.exp(spread * noise) if base else spread * noise
        out[name] = __import__('jax').numpy.asarray(drawn.astype(out[name].dtype))
    for name, factor in factors.items():
        out[name] = (out[name] * factor).astype(out[name].dtype)
    return out
```

```python
import math
from contextlib import ExitStack

import concourse.bass as bass
from concourse import mybir
import numpy as np

P = 128
D = 1024
T = 256
TT = T // P
KT = D // P
HEADS, KV, HD = 16, 4, 64
PAIRS = HEADS // 2
QT = PAIRS + KV // 2
TAPS, HALF_TAPS = 31, 15
FF = 3584
FB = FF // 512
EXPERTS = 8
BANK = 512
PANEL = 2048
RAW, SPLIT = 7, 3
PER_FFN = 6 * FB
LN_EPS = 1e-5
ALPHA = 4.0 ** 0.25
DVE_TILES, PE_TILES = (0, 1, 2, 3, 4), (5, 6, 7)
TAP_GROUP = 4

N_QKV = 0
N_WO = N_QKV + 6
N_FFN = N_WO + 4
N_PW1 = N_FFN + PER_FFN
N_PW2 = N_PW1 + 8
N_MOE = N_PW2 + 4

C_ID, C_TRI, C_ONE, C_IOTA = 0, 128, 256, 384
C_MASK = C_IOTA + 256
C_COS = C_MASK + 512
C_SIN = C_COS + TT * 32
C_NSIN = C_SIN + TT * 32
C_END = C_NSIN + TT * 32


def build(nc, x, attn_w_qkv, attn_sink, attn_w_o, conv_pw1_w, conv_pw1_b, conv_dw_w, conv_dw_b,
          conv_norm_g, conv_norm_b, conv_pw2_w, conv_pw2_b, ffn_w_gate, ffn_w_up, ffn_w_down,
          moe_router, moe_w_gate, moe_w_up, moe_w_down, ln_mix_g, ln_mix_b, ln_ffn_g, ln_ffn_b,
          shape_consts, out):
    fp32, f32r = mybir.dt.float32, mybir.dt.float32r
    u32, i32 = mybir.dt.uint32, mybir.dt.int32
    ALU, ACT, AX = mybir.AluOpType, mybir.ActivationFunctionType, mybir.AxisListType
    ctx = ExitStack()

    def sb(name, shape, dt=fp32, where=ctx):
        return where.enter_context(nc.sbuf_tensor(name, shape, dt))

    def sem(name):
        return ctx.enter_context(nc.semaphore(name))

    with ctx:
        raw = sb("raw", [P, RAW, PANEL])
        w_hi = sb("w_hi", [P, SPLIT, PANEL], f32r)
        w_lo = sb("w_lo", [P, SPLIT, PANEL], f32r)
        X = sb("X", [P, TT, D])
        xT_hi = sb("xT_hi", [P, KT, T], f32r)
        xT_lo = sb("xT_lo", [P, KT, T], f32r)
        consts = sb("consts", [P, C_END])
        ln_gb = sb("ln_gb", [P, 2, D])
        stats = sb("stats", [P, TT, 2, 6])
        mean_var = sb("mean_var", [P, TT, 2])
        var_eps = sb("var_eps", [P, TT])
        rstd = sb("rstd", [P, TT])
        minus_half = sb("minus_half", [P, T])
        router = sb("router", [P, KT, EXPERTS])
        psum = ctx.enter_context(nc.psum_tensor("psum", [P, 8, BANK], fp32))
        ident = consts[:, C_ID:C_ID + P]
        ones = consts[:, C_ONE:C_ONE + P]
        tri = consts[:, C_TRI:C_TRI + P]

        attn = ExitStack()
        sink = sb("sink", [P, HEADS], where=attn)
        rope_cos = sb("rope_cos", [P, 2, BANK], where=attn)
        rope_sin = sb("rope_sin", [P, 2, BANK], where=attn)
        roped = sb("roped", [P, TT, QT, P], where=attn)
        qkT = sb("qkT", [P, QT, T], where=attn)
        v = sb("v", [P, TT, KV * HD], where=attn)
        probs = sb("probs", [P, 2, 4, T], where=attn)
        pT = sb("pT", [P, 2, TT, T], where=attn)
        row_max = sb("row_max", [P, 2, 4], where=attn)
        neg_max = sb("neg_max", [P, 2, 4], where=attn)
        sink_arg = sb("sink_arg", [P, 2, 4], where=attn)
        sink_exp = sb("sink_exp", [P, 2, 4], where=attn)
        row_sum = sb("row_sum", [P, 2, 4], where=attn)
        denom = sb("denom", [P, 2, 4], where=attn)
        inv_denom = sb("inv_denom", [P, 2, 4], where=attn)
        attn.close()

        conv = ExitStack()
        conv_rows = sb("conv_rows", [40, P], where=conv)
        tap_rows = sb("tap_rows", [32, D], where=conv)
        conv_cols = sb("conv_cols", [P, 40], where=conv)
        taps = sb("taps", [P, KT, 32], where=conv)
        sig = sb("sig", [P, 4, T], where=conv)
        glu = sb("glu", [P, KT, T + 2 * HALF_TAPS + 2], where=conv)
        cv = sb("cv", [P, KT, T], where=conv)
        cv_sq = sb("cv_sq", [P, KT, T], where=conv)
        cv_var = sb("cv_var", [P, T], where=conv)
        cv_rstd = sb("cv_rstd", [P, T], where=conv)
        diag = sb("diag", [P, TAP_GROUP, P], where=conv)
        pw2_b = sb("pw2_b", [P, D], where=conv)
        mean_w = sb("mean_w", [P, P], where=conv)
        conv.close()

        h_silu = sb("h_silu", [P, TT, BANK])
        h = sb("h", [P, TT, BANK])
        hT_hi = sb("hT_hi", [P, 4, T], f32r)
        hT_lo = sb("hT_lo", [P, 4, T], f32r)
        xg_hi = sb("xg_hi", [P, KT, P], f32r)
        xg_lo = sb("xg_lo", [P, KT, P], f32r)
        ye = sb("ye", [P, D])
        y_acc = sb("y_acc", [P, TT, D])
        pick = sb("pick", [P, TT, P])
        place = sb("place", [P, TT, P])
        placeT = sb("placeT", [P, T])
        logits = sb("logits", [P, TT, EXPERTS])
        top_val = sb("top_val", [P, TT, EXPERTS])
        top_idx = sb("top_idx", [P, TT, EXPERTS], u32)
        top_idx_f = sb("top_idx_f", [P, TT, EXPERTS])
        gate_arg = sb("gate_arg", [P, TT])
        gate_exp = sb("gate_exp", [P, TT])
        gates = sb("gates", [P, TT, 2])
        combine = sb("combine", [P, TT, EXPERTS])
        combine2 = sb("combine2", [P, TT, EXPERTS])
        chosen = sb("chosen", [P, TT, EXPERTS])
        chosen2 = sb("chosen2", [P, TT, EXPERTS])
        slot = sb("slot", [P, TT, EXPERTS + 1])
        most = sb("most", [1, 2])
        overflow = sb("overflow", [1, 1], i32)
        join = sb("join", [1, 4])

        landed = [sem(f"landed{i}") for i in range(RAW)]
        hi_ready = sem("hi_ready")
        lo_ready = sem("lo_ready")
        panel_used = sem("panel_used")
        x_in = sem("x_in")
        consts_in = sem("consts_in")
        sink_in = sem("sink_in")
        gb_in = sem("gb_in")
        conv_in = sem("conv_in")
        router_in = sem("router_in")
        out_done = sem("out_done")
        dve_done = sem("dve_done")
        half_set = sem("half_set")
        x_ready = sem("x_ready")
        normed = sem("normed")
        var_ready = sem("var_ready")
        rstd_ready = sem("rstd_ready")
        xT_psum, xT_hi_ready, xT_lo_ready = sem("xT_psum"), sem("xT_hi_ready"), sem("xT_lo_ready")
        rope_terms, rope_added, v_ready = sem("rope_terms"), sem("rope_added"), sem("v_ready")
        qkT_psum, qkT_act, qkT_dve = sem("qkT_psum"), sem("qkT_act"), sem("qkT_dve")
        scores, masked, maxed, exped = sem("scores"), sem("masked"), sem("maxed"), sem("exped")
        inv_ready, probs_ready = sem("inv_ready"), sem("probs_ready")
        pT_psum, pT_act, pT_dve = sem("pT_psum"), sem("pT_act"), sem("pT_dve")
        o_psum, o_hi, o_lo = sem("o_psum"), sem("o_hi"), sem("o_lo")
        silu_done, h_ready = sem("silu_done"), sem("h_ready")
        hT_psum, hT_hi_ready, hT_lo_ready = sem("hT_psum"), sem("hT_hi_ready"), sem("hT_lo_ready")
        pads_zero, conv_colsT, taps_ready = sem("pads_zero"), sem("conv_colsT"), sem("taps_ready")
        sig_done, glu_done = sem("sig_done"), sem("glu_done")
        diag_ready, diag_used = sem("diag_ready"), sem("diag_used")
        conv_act, conv_dve = sem("conv_act"), sem("conv_dve")
        mean_psum, centred, squared, cvar_psum = sem("mean_psum"), sem("centred"), sem("squared"), sem("cvar_psum")
        cvar_ready, crstd_ready, scaled = sem("cvar_ready"), sem("crstd_ready"), sem("scaled")
        act_out, z_hi, z_lo = sem("act_out"), sem("z_hi"), sem("z_lo")
        x_scaled = sem("x_scaled")
        logits_psum, gate_arg_ready, gate_exp_ready = sem("logits_psum"), sem("gate_arg_ready"), sem("gate_exp_ready")
        chosen_ready, slot_psum, routed = sem("chosen_ready"), sem("slot_psum"), sem("routed")
        moe_zero = sem("moe_zero")
        pick_ready, place_ready = sem("pick_ready"), sem("place_ready")
        xg_psum, xg_hi_ready, xg_lo_ready = sem("xg_psum"), sem("xg_hi_ready"), sem("xg_lo_ready")
        ye_ready, placeT_psum, placeT_ready = sem("ye_ready"), sem("placeT_psum"), sem("placeT_ready")
        scattered, y_added = sem("scattered"), sem("y_added")
        passes_act, passes_dve, last_scatter = sem("passes_act"), sem("passes_dve"), sem("last_scatter")

        assert PER_FFN % RAW == 0 and PER_FFN % SPLIT == 0
        dmas_before = [0] * (N_MOE + 1)
        seen = [0] * RAW
        for n in range(N_MOE):
            seen[n % RAW] += 2 if N_WO <= n < N_WO + 4 else 1
            dmas_before[n] = seen[n % RAW]

        def number(n0, e):
            return n0 if e is None else e * PER_FFN + n0

        def landed_at(n0, e):
            if n0 < N_MOE:
                return 16 * dmas_before[n0]
            turns = seen[n0 % RAW] + 1 + (n0 - N_MOE) // RAW
            return e * (16 * PER_FFN // RAW) + 16 * turns

        def wide(w, half, c):
            return w[half * 512:half * 512 + 512, c * 512:c * 512 + 512].rearrange("(k p) n -> p k n", p=P)

        def tall(w, i):
            return w[i * 256:i * 256 + 256, :].rearrange("(k p) n -> p k n", p=P)

        def raw_as(n0, k):
            return raw[:, n0 % RAW, :].rearrange("p (k n) -> p k n", k=k)

        def ffn_panels():
            for j in range(FB):
                for kind in ("gate", "up"):
                    for half in range(2):
                        yield kind, j, half
                if j:
                    for half in range(2):
                        yield "down", j - 1, half
            for half in range(2):
                yield "down", FB - 1, half

        FFN_AT = {what: k for k, what in enumerate(ffn_panels())}

        G_B, U_B = (0, 1), (2, 3)
        EG_B, EU_B, EY_B = (0,), (1,), (2, 3)

        def bank(i, a=0, b=BANK):
            return psum[:, i, a:b]

        def heads_view(ap):
            return ap.rearrange("p (h s d) -> p h s d", s=2, d=HD // 2)

        def rope_table(col, tt, n):
            t = consts[:, col + tt * 32:col + tt * 32 + 32]
            return t.unsqueeze(1).unsqueeze(1).broadcast_to([P, n, 2, 32]) if col == C_COS else \
                t.unsqueeze(1).broadcast_to([P, n, 32])

        block = ctx.enter_context(nc.Block())

        @block.sync
        def _(sp):
            def load(n0, e, dst_src):
                if n0 >= RAW:
                    sp.wait_ge(lo_ready, number(n0 - RAW + 1, e))
                for dst, src in dst_src:
                    sp.dma_start(dst, src).then_inc(landed[n0 % RAW], 16)

            def load_ffn(first, e, w_gate, w_up, w_down):
                for k, (kind, j, half) in enumerate(ffn_panels()):
                    if kind == "down":
                        src, dst = tall(w_down, 2 * j + half), raw_as(first + k, 2)
                    else:
                        src, dst = wide(w_gate if kind == "gate" else w_up, half, j), raw_as(first + k, 4)
                    load(first + k, e, [(dst, src)])

            sp.dma_start(X[:, :, :], x[0].rearrange("(t p) d -> p t d", p=P)).then_inc(x_in, 16)
            sp.dma_start(consts[:, :], shape_consts).then_inc(consts_in, 16)
            for c in range(3):
                for half in range(2):
                    n = N_QKV + 2 * c + half
                    load(n, None, [(raw_as(n, 4), wide(attn_w_qkv[0], half, c))])
            wo = attn_w_o[0].rearrange("(kv g d) n -> kv d g n", kv=KV, d=HD)
            for i in range(4):
                n = N_WO + i
                load(n, None, [(raw_as(n, 2)[HD * b:HD * b + HD], wo[2 * (i // 2) + b][:, 2 * (i % 2):2 * (i % 2) + 2, :])
                               for b in range(2)])
            load_ffn(N_FFN, None, ffn_w_gate[0], ffn_w_up[0], ffn_w_down[0])
            for i, c in enumerate((2, 0, 3, 1)):
                for half in range(2):
                    n = N_PW1 + 2 * i + half
                    load(n, None, [(raw_as(n, 4), wide(conv_pw1_w[0], half, c))])
            for i in range(4):
                load(N_PW2 + i, None, [(raw_as(N_PW2 + i, 2), tall(conv_pw2_w[0], i))])

            def experts(p):
                with sp.Fori(EXPERTS * p, EXPERTS * (p + 1)) as e:
                    i = e - EXPERTS * p
                    load_ffn(N_MOE, e, moe_w_gate[0, bass.ds(i, 1)][0], moe_w_up[0, bass.ds(i, 1)][0],
                             moe_w_down[0, bass.ds(i, 1)][0])

            experts(0)
            sp.wait_ge(routed, 1)
            again = sp.value_load(overflow[0:1, 0:1], min_val=0, max_val=1)
            with sp.If(again > 0):
                experts(1)
            sp.wait_ge(x_ready, 16)
            sp.dma_start(out[0].rearrange("(t p) d -> p t d", p=P), X[:, :, :]).then_inc(out_done, 16)
            sp.wait_ge(out_done, 16)

        @block.gpsimd
        def _(pool):
            pool.dma_start(sink[:, :], attn_sink[0].partition_broadcast(P)).then_inc(sink_in, 16)

            def load_norm(i, g, b):
                if i:
                    pool.wait_ge(x_ready, 4 * i)
                pool.dma_start(ln_gb[:, 0, :], g.partition_broadcast(P)).then_inc(gb_in, 16)
                pool.dma_start(ln_gb[:, 1, :], b.partition_broadcast(P)).then_inc(gb_in, 16)

            load_norm(0, ln_mix_g[0], ln_mix_b[0])
            nc.gpsimd.memset(minus_half[:, :], -0.5).then_inc(half_set, 1)

            for c in range(3):
                for tt in range(TT):
                    i = 2 * c + tt
                    pool.wait_ge(rope_terms, i + 1)
                    n = 4 if c == 2 else 8
                    a, b = rope_cos[:, i % 2, 0:n * HD], rope_sin[:, i % 2, 0:n * HD]
                    if c == 2:
                        o = roped[:, tt, PAIRS:QT, :].rearrange("p a n -> p (a n)")
                    else:
                        a = a.rearrange("p (b g d) -> p b g d", b=2, d=HD)
                        b = b.rearrange("p (b g d) -> p b g d", b=2, d=HD)
                        o = roped[:, tt, 4 * c:4 * c + 4, :].rearrange("p g (b d) -> p b g d", b=2)
                    nc.gpsimd.tensor_tensor(o, a, b, ALU.add).then_inc(rope_added, 1)

            for j in range(PAIRS):
                pool.wait_ge(inv_ready, j + 1)
                for i in range(4):
                    last = nc.gpsimd.tensor_scalar(probs[:, j % 2, i, :], probs[:, j % 2, i, :],
                                                   inv_denom[:, j % 2, i:i + 1], None, ALU.mult)
                last.then_inc(probs_ready, 1)

            def norm_tail(i):
                pool.wait_ge(half_set, 1)
                for tt in range(TT):
                    pool.wait_ge(var_ready, 2 * i + tt + 1)
                    nc.gpsimd.tensor_tensor(rstd[:, tt:tt + 1], var_eps[:, tt:tt + 1],
                                            minus_half[:, tt:tt + 1], ALU.pow).then_inc(rstd_ready, 1)
                pool.wait_ge(gb_in, 32 * (i + 1))
                for half in range(2):
                    for tt in range(TT):
                        s = slice(512 * half, 512 * half + 512)
                        pool.wait_ge(normed, 4 * i + 2 * half + tt + 1)
                        nc.gpsimd.tensor_tensor(X[:, tt, s], X[:, tt, s], ln_gb[:, 1, s], ALU.add).then_inc(x_ready, 1)

            norm_tail(0)
            load_norm(1, ln_ffn_g[0], ln_ffn_b[0])
            norm_tail(1)
            load_norm(2, ln_mix_g[1], ln_mix_b[1])
            nc.gpsimd.memset(glu[:, :, :], 0.0).then_inc(pads_zero, 1)
            nc.gpsimd.memset(tap_rows[:, :], 0.0).then_inc(pads_zero, 1)
            nc.gpsimd.memset(mean_w[:, :], 1.0 / D).then_inc(pads_zero, 1)
            pool.wait_ge(pads_zero, 2)
            pool.dma_start(tap_rows[0:TAPS, :], conv_dw_w[0]).then_inc(conv_in, 16)
            for at, vec in ((0, conv_pw1_b), (16, conv_dw_b), (24, conv_norm_g), (32, conv_norm_b)):
                rows = vec.shape[1] // P
                pool.dma_start(conv_rows[at:at + rows, :], vec[0].rearrange("(r c) -> r c", c=P)).then_inc(conv_in, 16)
            pool.dma_start(pw2_b[:, :], conv_pw2_b[0].partition_broadcast(P)).then_inc(conv_in, 16)
            pool.dma_start(router[:, :, :], moe_router[0].rearrange("(k p) e -> p k e", p=P)).then_inc(router_in, 16)
            pool.wait_ge(xT_psum, 12)
            nc.gpsimd.tensor_scalar(X[:, :, :], X[:, :, :], ALPHA, None, ALU.mult).then_inc(x_scaled, 1)
            pool.wait_ge(x_scaled, 1)
            pool.wait_ge(conv_in, 96)
            for tt in range(TT):
                nc.gpsimd.tensor_tensor(X[:, tt, :], X[:, tt, :], pw2_b[:, :], ALU.add).then_inc(x_scaled, 1)
            pool.wait_ge(cvar_ready, 1)
            nc.gpsimd.tensor_tensor(cv_rstd[:, :], cv_var[:, :], minus_half[:, :], ALU.pow).then_inc(crstd_ready, 1)
            norm_tail(2)
            load_norm(3, ln_ffn_g[1], ln_ffn_b[1])
            nc.gpsimd.memset(y_acc[:, :, :], 0.0).then_inc(moe_zero, 1)
            nc.gpsimd.memset(ye[:, :], 0.0).then_inc(moe_zero, 1)
            nc.gpsimd.memset(placeT[:, :], 0.0).then_inc(moe_zero, 1)
            nc.gpsimd.memset(slot[:, :, :], -1.0).then_inc(moe_zero, 1)
            norm_tail(3)

        @block.scalar
        def _(act):
            def round_panel(n0, e=None):
                act.wait_ge(landed[n0 % RAW], landed_at(n0, e))
                if n0 >= SPLIT:
                    act.wait_ge(panel_used, number(n0 - SPLIT + 1, e))
                nc.scalar.activation(w_hi[:, n0 % SPLIT, :], raw[:, n0 % RAW, :], ACT.Copy).then_inc(hi_ready, 1)

            def round_xT(r):
                for b in range(4):
                    act.wait_ge(xT_psum, 4 * r + b + 1)
                    nc.scalar.activation(xT_hi[:, 2 * b:2 * b + 2, :].rearrange("p k t -> p (k t)"), bank(4 + b),
                                         ACT.Copy).then_inc(xT_hi_ready, 1)

            round_panel(0)
            round_xT(0)
            for n in range(1, 6):
                round_panel(n)
            for tt in range(TT):
                act.wait_ge(rope_terms, 5 + tt)
                nc.scalar.activation(v[:, tt, :], bank(4 + tt, 256), ACT.Copy).then_inc(v_ready, 1)
            for b in (0, 2, 4):
                act.wait_ge(qkT_psum, b + 1)
                nc.scalar.activation(qkT[:, 2 * b:2 * b + 2, :].rearrange("p k t -> p (k t)"), bank(b),
                                     ACT.Copy).then_inc(qkT_act, 1)

            for s in range(PAIRS + 2):
                if s < PAIRS:
                    act.wait_ge(maxed, s + 1)
                    if s >= 2:
                        act.wait_ge(inv_ready, s - 1)
                    for i in range(4):
                        nc.scalar.activation(probs[:, s % 2, i, :], probs[:, s % 2, i, :], ACT.Exp,
                                             bias=neg_max[:, s % 2, i:i + 1], accum_out=row_sum[:, s % 2, i:i + 1])
                    nc.scalar.activation(sink_exp[:, s % 2, :], sink_arg[:, s % 2, :], ACT.Exp).then_inc(exped, 1)
                if 1 <= s < PAIRS + 1:
                    act.wait_ge(pT_psum, s)
                    if s >= 2:
                        act.wait_ge(o_psum, s - 1)
                    nc.scalar.activation(pT[:, 0, :, :].rearrange("p k t -> p (k t)"), bank(4),
                                         ACT.Copy).then_inc(pT_act, 1)
                if s >= 2:
                    j = s - 2
                    act.wait_ge(o_psum, j + 1)
                    nc.scalar.activation(xT_hi[:, j, :], bank(6 + j % 2, 0, T), ACT.Copy).then_inc(o_hi, 1)

            for n in range(N_WO, N_WO + 4):
                round_panel(n)
            round_panel(N_FFN)
            round_xT(1)

            def swiglu(first, e, nt, q0, per, gb, extra=None):
                def q(j, tt):
                    k = q0 + nt * j + tt
                    return k if e is None else e * per + k

                def panel(kind, j, half):
                    if e is None and kind == "gate" and j == 0 and half == 0:
                        return
                    round_panel(first + FFN_AT[kind, j, half], e)

                def round_hT(j):
                    for tt in range(nt):
                        act.wait_ge(hT_psum, q(j, tt) + 1)
                        nc.scalar.activation(hT_hi[:, :, tt * P:tt * P + P],
                                             bank((U_B if nt == 2 else EU_B)[tt]).rearrange("p (k t) -> p k t", k=4),
                                             ACT.Copy).then_inc(hT_hi_ready, 1)

                for j in range(FB):
                    panel("gate", j, 0)
                    if j:
                        round_hT(j - 1)
                    if extra:
                        extra(j)
                    panel("gate", j, 1)
                    panel("up", j, 0)
                    panel("up", j, 1)
                    act.wait_ge(panel_used, number(first + FFN_AT["gate", j, 1] + 1, e))
                    for tt in range(nt):
                        if e is not None or j:
                            act.wait_ge(h_ready, q(j, tt) - nt + 1)
                        nc.scalar.activation(h_silu[:, tt, :], bank(gb[tt]), ACT.Silu).then_inc(silu_done, 1)
                    if j:
                        panel("down", j - 1, 0)
                        panel("down", j - 1, 1)
                if extra:
                    extra(FB)
                panel("down", FB - 1, 0)
                round_hT(FB - 1)
                panel("down", FB - 1, 1)

            swiglu(N_FFN, None, TT, 0, 0, G_B)
            round_panel(N_PW1)
            act.wait_ge(conv_colsT, 1)
            nc.scalar.activation(conv_cols[:, :], bank(0, 0, 40), ACT.Copy).then_inc(taps_ready, 1)
            nc.scalar.activation(taps[:, :, :].rearrange("p k t -> p (k t)"), bank(1, 0, KT * 32),
                                 ACT.Copy).then_inc(taps_ready, 1)
            round_xT(2)
            act.wait_ge(taps_ready, 2)
            for n in range(N_PW1 + 1, N_PW1 + 8):
                round_panel(n)
                if n in (N_PW1 + 2, N_PW1 + 6):
                    c = (n - N_PW1) // 4
                    act.wait_ge(panel_used, n)
                    if c:
                        act.wait_ge(glu_done, 4)
                    for m in range(4):
                        col = 8 + 4 * c + m
                        nc.scalar.activation(sig[:, m, :], bank(m, 0, T), ACT.Sigmoid,
                                             bias=conv_cols[:, col:col + 1]).then_inc(sig_done, 1)
            for t, m in enumerate(PE_TILES):
                def diagonal(i, tap, group):
                    if t or group is not None:
                        before = (32 * t if group is None else group * TAP_GROUP + 32 * t) + i + 1 - TAP_GROUP
                        act.wait_ge(diag_used, before)
                    nc.scalar.activation(diag[:, i, :], ident, ACT.Copy, scale=tap).then_inc(diag_ready, 1)

                for i in range(TAP_GROUP):
                    diagonal(i, taps[:, m, i:i + 1], None)
                with act.Fori(1, 32 // TAP_GROUP) as group:
                    for i in range(TAP_GROUP):
                        diagonal(i, taps[:, m, bass.ds(group * TAP_GROUP + i, 1)], group)
            for t, m in enumerate(PE_TILES):
                act.wait_ge(diag_used, 32 * (t + 1))
                nc.scalar.activation(cv[:, m, :], bank(t, 0, T), ACT.Identity,
                                     bias=conv_cols[:, 16 + m:17 + m]).then_inc(conv_act, 1)
            act.wait_ge(centred, 1)
            nc.scalar.activation(cv_sq[:, :, :], cv[:, :, :], ACT.Square).then_inc(squared, 1)
            act.wait_ge(scaled, 1)
            for m in range(KT):
                nc.scalar.activation(cv_sq[:, m, :], cv[:, m, :], ACT.Silu, scale=conv_cols[:, 24 + m:25 + m],
                                     bias=conv_cols[:, 32 + m:33 + m]).then_inc(act_out, 1)
            for i in range(2):
                act.wait_ge(act_out, 4 * i + 4)
                nc.scalar.activation(xT_hi[:, 4 * i:4 * i + 4, :], cv_sq[:, 4 * i:4 * i + 4, :], ACT.Copy).then_inc(z_hi, 1)
            for n in range(N_PW2, N_PW2 + 4):
                round_panel(n)
            round_xT(3)
            act.wait_ge(gate_arg_ready, 1)
            nc.scalar.activation(gate_exp[:, :], gate_arg[:, :], ACT.Exp).then_inc(gate_exp_ready, 1)

            def round_gathered(turn):
                act.wait_ge(xg_psum, turn + 1)
                for i in range(2):
                    nc.scalar.activation(xg_hi[:, 4 * i:4 * i + 4, :].rearrange("p k t -> p (k t)"), bank(4 + i),
                                         ACT.Copy).then_inc(xg_hi_ready, 1)

            def experts(p):
                round_gathered(9 * p)
                with act.Fori(EXPERTS * p, EXPERTS * (p + 1)) as e:
                    def extra(j):
                        if j == 4:
                            act.wait_ge(placeT_psum, e + 1)
                            act.wait_ge(moe_zero, 4)
                            nc.scalar.activation(placeT[:, :], bank(6, 0, T), ACT.Copy).then_inc(placeT_ready, 1)
                        if j == FB:
                            round_gathered(e + (1 + p))

                    swiglu(N_MOE, e, 1, TT * FB, FB, EG_B, extra)
                    act.wait_ge(panel_used, number(N_MOE + PER_FFN, e))
                    for half in range(2):
                        nc.scalar.activation(ye[:, 512 * half:512 * half + 512], bank(EY_B[half]),
                                             ACT.Copy).then_inc(ye_ready, 1)

            experts(0)
            act.wait_ge(routed, 1)
            again = act.value_load(overflow[0:1, 0:1], min_val=0, max_val=1)
            with act.If(again > 0):
                experts(1)
            nc.scalar.activation(join[:, 0:1], minus_half[0:1, 0:1], ACT.Copy).then_inc(passes_act, 1)

        @block.vector
        def _(dve):
            steps = [0]

            def step(ins):
                steps[0] += 1
                ins.then_inc(dve_done, 1)
                dve.wait_ge(dve_done, steps[0])

            def rest_panel(n0, e=None):
                dve.wait_ge(hi_ready, number(n0 + 1, e))
                if n0 >= SPLIT:
                    dve.wait_ge(panel_used, number(n0 - SPLIT + 1, e))
                nc.vector.tensor_tensor(w_lo[:, n0 % SPLIT, :], raw[:, n0 % RAW, :],
                                        w_hi[:, n0 % SPLIT, :].bitcast(fp32), ALU.subtract).then_inc(lo_ready, 1)

            def rest_xT(r):
                for b in range(4):
                    dve.wait_ge(xT_hi_ready, 4 * r + b + 1)
                    d = slice(2 * b, 2 * b + 2)
                    nc.vector.tensor_tensor(xT_lo[:, d, :].rearrange("p k t -> p (k t)"), bank(4 + b),
                                            xT_hi[:, d, :].rearrange("p k t -> p (k t)").bitcast(fp32),
                                            ALU.subtract).then_inc(xT_lo_ready, 1)

            rest_panel(0)
            rest_xT(0)
            for n in range(1, 6):
                rest_panel(n)
            dve.wait_ge(consts_in, 16)
            for c in range(3):
                dve.wait_ge(panel_used, 2 * c + 2)
                for tt in range(TT):
                    i = 2 * c + tt
                    n = 4 if c == 2 else 8
                    src = heads_view(bank(2 * c + tt, 0, n * HD))
                    if i >= 2:
                        dve.wait_ge(rope_added, i - 1)
                    nc.vector.tensor_tensor(heads_view(rope_cos[:, i % 2, 0:n * HD]), src,
                                            rope_table(C_COS, tt, n), ALU.mult)
                    dst = heads_view(rope_sin[:, i % 2, 0:n * HD])
                    nc.vector.tensor_tensor(dst[:, :, 0, :], src[:, :, 1, :], rope_table(C_NSIN, tt, n), ALU.mult)
                    nc.vector.tensor_tensor(dst[:, :, 1, :], src[:, :, 0, :], rope_table(C_SIN, tt, n),
                                            ALU.mult).then_inc(rope_terms, 1)
            for b in (1, 3):
                dve.wait_ge(qkT_psum, b + 1)
                nc.vector.tensor_copy(qkT[:, 2 * b:2 * b + 2, :].rearrange("p k t -> p (k t)"),
                                      bank(b)).then_inc(qkT_dve, 1)
            dve.wait_ge(sink_in, 16)
            mask = consts[:, C_MASK:C_MASK + 512].unsqueeze(1).broadcast_to([P, 2, 512])
            for s in range(PAIRS + 2):
                if s < PAIRS:
                    k = s % 2
                    dve.wait_ge(scores, s + 1)
                    if s >= 2:
                        dve.wait_ge(pT_psum, s - 1)
                    nc.vector.scalar_tensor_tensor(
                        probs[:, k, :, :].rearrange("p (b q) t -> p b (q t)", b=2), psum[:, 2 * k:2 * k + 2, :],
                        HD ** -0.5, mask, ALU.mult, ALU.add).then_inc(masked, 1)
                    dve.wait_ge(masked, s + 1)
                    step(nc.vector.reduce_max(row_max[:, k, :], probs[:, k, :, :], AX.X))
                    first = (2 * (s // 4)) * 4 + s % 4
                    sinks = sink[:, first:first + 5:4].unsqueeze(2).broadcast_to([P, 2, 2])
                    by_head = lambda t: t[:, k, :].rearrange("p (b q) -> p b q", b=2)
                    step(nc.vector.tensor_tensor(by_head(row_max), by_head(row_max), sinks, ALU.max))
                    step(nc.vector.tensor_scalar(neg_max[:, k, :], row_max[:, k, :], -1.0, None, ALU.mult))
                    nc.vector.tensor_tensor(by_head(sink_arg), by_head(neg_max), sinks, ALU.add).then_inc(maxed, 1)
                if 1 <= s < PAIRS + 1:
                    dve.wait_ge(pT_psum, s)
                    if s >= 2:
                        dve.wait_ge(o_psum, s - 1)
                    nc.vector.tensor_copy(pT[:, 1, :, :].rearrange("p k t -> p (k t)"), bank(5)).then_inc(pT_dve, 1)
                if s < PAIRS:
                    dve.wait_ge(exped, s + 1)
                    step(nc.vector.tensor_tensor(denom[:, k, :], row_sum[:, k, :], sink_exp[:, k, :], ALU.add))
                    if s >= 2:
                        dve.wait_ge(probs_ready, s - 1)
                    nc.vector.reciprocal(inv_denom[:, k, :], denom[:, k, :]).then_inc(inv_ready, 1)
                if s >= 2:
                    j = s - 2
                    dve.wait_ge(o_hi, j + 1)
                    nc.vector.tensor_tensor(xT_lo[:, j, :], bank(6 + j % 2, 0, T), xT_hi[:, j, :].bitcast(fp32),
                                            ALU.subtract).then_inc(o_lo, 1)
            for n in range(N_WO, N_WO + 4):
                rest_panel(n)
            rest_panel(N_FFN)

            def layer_norm(i, mix, alpha):
                halves = [slice(512 * k, 512 * k + 512) for k in range(2)]
                for tt in range(TT):
                    for k, s in enumerate(halves):
                        step(nc.vector.scalar_tensor_tensor(X[:, tt, s], X[:, tt, s], alpha, mix(tt, k),
                                                            ALU.mult, ALU.add))
                        nc.vector.bn_stats(stats[:, tt, k, :], X[:, tt, s]).then_inc(dve_done, 1)
                        steps[0] += 1
                    dve.wait_ge(dve_done, steps[0])
                    step(nc.vector.bn_aggr(mean_var[:, tt, :], stats[:, tt, :, :].rearrange("p k s -> p (k s)")))
                    nc.vector.tensor_scalar(var_eps[:, tt:tt + 1], mean_var[:, tt, 1:2], LN_EPS, None,
                                            ALU.add).then_inc(var_ready, 1)
                for tt in range(TT):
                    dve.wait_ge(rstd_ready, 2 * i + tt + 1)
                    step(nc.vector.tensor_scalar(X[:, tt, :], X[:, tt, :], mean_var[:, tt, 0:1], rstd[:, tt:tt + 1],
                                                 ALU.subtract, ALU.mult))
                dve.wait_ge(gb_in, 32 * (i + 1))
                for s in halves:
                    for tt in range(TT):
                        nc.vector.tensor_tensor(X[:, tt, s], X[:, tt, s], ln_gb[:, 0, s], ALU.mult).then_inc(normed, 1)

            dve.wait_ge(panel_used, N_WO + 4)
            layer_norm(0, lambda tt, k: bank(2 * tt + k), ALPHA)
            rest_xT(1)

            def swiglu(first, e, nt, q0, per, gb, ub, extra=None):
                def q(j, tt):
                    k = q0 + nt * j + tt
                    return k if e is None else e * per + k

                def panel(kind, j, half):
                    if e is None and kind == "gate" and j == 0 and half == 0:
                        return
                    rest_panel(first + FFN_AT[kind, j, half], e)

                def rest_hT(j):
                    for tt in range(nt):
                        dve.wait_ge(hT_hi_ready, q(j, tt) + 1)
                        nc.vector.tensor_tensor(hT_lo[:, :, tt * P:tt * P + P],
                                                bank(ub[tt]).rearrange("p (k t) -> p k t", k=4),
                                                hT_hi[:, :, tt * P:tt * P + P].bitcast(fp32),
                                                ALU.subtract).then_inc(hT_lo_ready, 1)

                for j in range(FB):
                    panel("gate", j, 0)
                    if j:
                        rest_hT(j - 1)
                    if extra:
                        extra(j)
                    panel("gate", j, 1)
                    panel("up", j, 0)
                    panel("up", j, 1)
                    if j:
                        panel("down", j - 1, 0)
                        panel("down", j - 1, 1)
                    dve.wait_ge(panel_used, number(first + FFN_AT["up", j, 1] + 1, e))
                    for tt in range(nt):
                        dve.wait_ge(silu_done, q(j, tt) + 1)
                        if e is not None or j:
                            dve.wait_ge(hT_psum, q(j, tt) - nt + 1)
                        nc.vector.tensor_tensor(h[:, tt, :], h_silu[:, tt, :], bank(ub[tt]),
                                                ALU.mult).then_inc(h_ready, 1)
                if extra:
                    extra(FB)
                panel("down", FB - 1, 0)
                rest_hT(FB - 1)
                panel("down", FB - 1, 1)

            swiglu(N_FFN, None, TT, 0, 0, G_B, U_B)
            rest_panel(N_PW1)
            dve.wait_ge(panel_used, N_FFN + PER_FFN)
            layer_norm(1, lambda tt, k: bank(4 + 2 * tt + k), ALPHA)
            rest_xT(2)
            dve.wait_ge(taps_ready, 2)
            dve.wait_ge(pads_zero, 3)

            def gated(c):
                dve.wait_ge(panel_used, N_PW1 + 4 * c + 4)
                for m in range(4):
                    col = 4 * c + m
                    dve.wait_ge(sig_done, col + 1)
                    nc.vector.scalar_tensor_tensor(glu[:, col, HALF_TAPS:HALF_TAPS + T], bank(4 + m, 0, T),
                                                   conv_cols[:, col:col + 1], sig[:, m, :], ALU.add,
                                                   ALU.mult).then_inc(glu_done, 1)

            def convolve(tiles, done):
                for m in tiles:
                    nc.vector.tensor_scalar(cv[:, m, :], glu[:, m, 0:T], taps[:, m, 0:1], conv_cols[:, 16 + m:17 + m],
                                            ALU.mult, ALU.add).then_inc(conv_dve, 1)
                with dve.Fori(1, TAPS) as tap:
                    for i, m in enumerate(tiles):
                        dve.wait_ge(conv_dve, tap * len(tiles) + (done + i + 1 - len(tiles)))
                        nc.vector.scalar_tensor_tensor(cv[:, m, :], glu[:, m, bass.ds(tap, T)],
                                                       taps[:, m, bass.ds(tap, 1)], cv[:, m, :], ALU.mult,
                                                       ALU.add).then_inc(conv_dve, 1)

            for n in range(N_PW1 + 1, N_PW1 + 5):
                rest_panel(n)
            gated(0)
            for n in range(N_PW1 + 5, N_PW1 + 8):
                rest_panel(n)
            dve.wait_ge(glu_done, 4)
            gated(1)
            dve.wait_ge(glu_done, 8)
            convolve(DVE_TILES[:4], 0)
            convolve(DVE_TILES[4:], 4 * TAPS)
            dve.wait_ge(mean_psum, 1)
            nc.vector.tensor_tensor(cv[:, :, :], cv[:, :, :], bank(4, 0, T).unsqueeze(1).broadcast_to([P, KT, T]),
                                    ALU.subtract).then_inc(centred, 1)
            dve.wait_ge(cvar_psum, 1)
            nc.vector.tensor_scalar(cv_var[:, :], bank(5, 0, T), LN_EPS, None, ALU.add).then_inc(cvar_ready, 1)
            dve.wait_ge(crstd_ready, 1)
            nc.vector.tensor_tensor(cv[:, :, :], cv[:, :, :], cv_rstd[:, :].unsqueeze(1).broadcast_to([P, KT, T]),
                                    ALU.mult).then_inc(scaled, 1)
            for i in range(2):
                dve.wait_ge(z_hi, i + 1)
                nc.vector.tensor_tensor(xT_lo[:, 4 * i:4 * i + 4, :], cv_sq[:, 4 * i:4 * i + 4, :],
                                        xT_hi[:, 4 * i:4 * i + 4, :].bitcast(fp32), ALU.subtract).then_inc(z_lo, 1)
            for n in range(N_PW2, N_PW2 + 4):
                rest_panel(n)
            dve.wait_ge(panel_used, N_PW2 + 4)
            dve.wait_ge(x_scaled, 3)
            layer_norm(2, lambda tt, k: bank(2 * tt + k), 1.0)
            rest_xT(3)

            dve.wait_ge(logits_psum, 1)
            for tt in range(TT):
                step(nc.vector.tensor_copy(logits[:, tt, :], bank(tt, 0, EXPERTS)))
                step(nc.vector.max(top_val[:, tt, :], logits[:, tt, :]))
                step(nc.vector.max_index(top_idx[:, tt, :], top_val[:, tt, :], logits[:, tt, :]))
            step(nc.vector.tensor_copy(top_idx_f[:, :, :], top_idx[:, :, :]))
            nc.vector.tensor_tensor(gate_arg[:, :], top_val[:, :, 1], top_val[:, :, 0],
                                    ALU.subtract).then_inc(gate_arg_ready, 1)
            iota8 = consts[:, C_IOTA:C_IOTA + EXPERTS]
            for tt in range(TT):
                step(nc.vector.tensor_scalar(chosen2[:, tt, :], iota8, top_idx_f[:, tt, 1:2], None, ALU.is_equal))
                step(nc.vector.scalar_tensor_tensor(chosen[:, tt, :], iota8, top_idx_f[:, tt, 0:1], chosen2[:, tt, :],
                                                    ALU.is_equal, ALU.add))
            nc.vector.memset(most[:, :], 0.0).then_inc(chosen_ready, 1)
            dve.wait_ge(gate_exp_ready, 1)
            step(nc.vector.tensor_scalar(gate_arg[:, :], gate_exp[:, :], 1.0, None, ALU.add))
            step(nc.vector.reciprocal(gates[:, :, 0], gate_arg[:, :]))
            step(nc.vector.tensor_tensor(gates[:, :, 1], gates[:, :, 0], gate_exp[:, :], ALU.mult))
            for tt in range(TT):
                step(nc.vector.tensor_scalar(combine[:, tt, :], iota8, top_idx_f[:, tt, 0:1], gates[:, tt, 0:1],
                                             ALU.is_equal, ALU.mult))
                step(nc.vector.tensor_scalar(combine2[:, tt, :], iota8, top_idx_f[:, tt, 1:2], gates[:, tt, 1:2],
                                             ALU.is_equal, ALU.mult))
            step(nc.vector.tensor_tensor(combine[:, :, :], combine[:, :, :], combine2[:, :, :], ALU.add))
            dve.wait_ge(slot_psum, 1)
            dve.wait_ge(moe_zero, 4)
            for tt in range(TT):
                step(nc.vector.scalar_tensor_tensor(slot[:, tt, 0:EXPERTS], bank(2 + tt, 0, EXPERTS), 1.0,
                                                    chosen[:, tt, :], ALU.add, ALU.mult))
            step(nc.vector.tensor_scalar(slot[:, :, 0:EXPERTS], slot[:, :, 0:EXPERTS], -1.0, None, ALU.add))
            step(nc.vector.reduce_max(most[0:1, 0:1], psum[0:1, 4, 0:EXPERTS], AX.X))
            nc.vector.tensor_scalar(overflow[0:1, 0:1], most[0:1, 0:1], P + 0.5, None, ALU.is_gt).then_inc(routed, 1)

            def one_hot(p, e):
                for tt in range(TT):
                    last = nc.vector.tensor_scalar(pick[:, tt, :], consts[:, C_IOTA + P * p:C_IOTA + P * p + P],
                                                   slot[:, tt, e], None, ALU.is_equal)
                last.then_inc(pick_ready, 1)

            def rest_gathered(turn):
                for i in range(2):
                    dve.wait_ge(xg_hi_ready, 2 * turn + i + 1)
                    d = slice(4 * i, 4 * i + 4)
                    nc.vector.tensor_tensor(xg_lo[:, d, :].rearrange("p k t -> p (k t)"), bank(4 + i),
                                            xg_hi[:, d, :].rearrange("p k t -> p (k t)").bitcast(fp32),
                                            ALU.subtract).then_inc(xg_lo_ready, 1)

            def add_scattered():
                for tt in range(TT):
                    for k in range(2):
                        s = slice(512 * k, 512 * k + 512)
                        nc.vector.tensor_tensor(y_acc[:, tt, s], y_acc[:, tt, s], bank(4 + 2 * tt + k),
                                                ALU.add).then_inc(y_added, 1)

            def experts(p):
                if p:
                    dve.wait_ge(xg_psum, 9)
                one_hot(p, slice(0, 1))
                rest_gathered(9 * p)
                with dve.Fori(EXPERTS * p, EXPERTS * (p + 1)) as e:
                    i = e - EXPERTS * p

                    def extra(j):
                        if j == 0:
                            dve.wait_ge(xg_psum, e + (1 + p))
                            one_hot(p, bass.ds(i + 1, 1))
                            dve.wait_ge(placeT_psum, e)
                            for tt in range(TT):
                                last = nc.vector.tensor_scalar(place[:, tt, :],
                                                               consts[:, C_IOTA + P * p:C_IOTA + P * p + P],
                                                               slot[:, tt, bass.ds(i, 1)], combine[:, tt, bass.ds(i, 1)],
                                                               ALU.is_equal, ALU.mult)
                            last.then_inc(place_ready, 1)
                        if j == 3:
                            dve.wait_ge(scattered, e + 1)
                            dve.wait_ge(y_added, e * 4)
                            add_scattered()
                        if j == FB:
                            rest_gathered(e + (1 + p))

                    swiglu(N_MOE, e, 1, TT * FB, FB, EG_B, EU_B, extra)

            experts(0)
            again = dve.value_load(overflow[0:1, 0:1], min_val=0, max_val=1)
            with dve.If(again > 0):
                experts(1)
            step(nc.vector.tensor_copy(join[:, 1:2], minus_half[0:1, 0:1]))
            nc.vector.tensor_copy(join[:, 2:3], minus_half[0:1, 0:1]).then_inc(passes_dve, 1)
            dve.wait_ge(last_scatter, 1)
            for tt in range(TT):
                for k in range(2):
                    s = slice(512 * k, 512 * k + 512)
                    step(nc.vector.tensor_tensor(y_acc[:, tt, s], y_acc[:, tt, s], bank(4 + 2 * tt + k), ALU.add))
            layer_norm(3, lambda tt, k: y_acc[:, tt, 512 * k:512 * k + 512], ALPHA)

        @block.tensor
        def _(pe):
            def three_passes(o, st, mv, start, stop):
                nc.tensor.matmul(o, st[0], mv[0], start=start, stop=False)
                nc.tensor.matmul(o, st[0], mv[1], start=False, stop=False)
                return nc.tensor.matmul(o, st[1], mv[0], start=False, stop=stop)

            def both(hi, lo, *at):
                return hi[at], lo[at]

            def panel(n0, a, b):
                return w_hi[:, n0 % SPLIT, a:b], w_lo[:, n0 % SPLIT, a:b]

            def wide_panel(n0, e, half, banks, lhs):
                pe.wait_ge(lo_ready, number(n0 + 1, e))
                for tt, b in enumerate(banks):
                    for kk in range(4):
                        last = three_passes(bank(b), lhs(4 * half + kk, tt), panel(n0, 512 * kk, 512 * kk + 512),
                                            half == 0 and kk == 0, half == 1 and kk == 3)
                return last.then_inc(panel_used, 1)

            def tall_panel(n0, e, banks, lhs, start, stop):
                pe.wait_ge(lo_ready, number(n0 + 1, e))
                for tt, pair in enumerate(banks):
                    for kk in range(2):
                        for k, b in enumerate(pair):
                            at = D * kk + 512 * k
                            last = three_passes(bank(b), lhs(kk, tt), panel(n0, at, at + 512),
                                                start and kk == 0, stop and kk == 1)
                return last.then_inc(panel_used, 1)

            def x_cols(kt, tt):
                at = (slice(None), kt, slice(tt * P, tt * P + P))
                return xT_hi[at], xT_lo[at]

            def transpose_x(r):
                for b in range(4):
                    if r:
                        pe.wait_ge(x_ready, 4 * (r - 1) + (2 if b < 2 else 4))
                    for kt in (2 * b, 2 * b + 1):
                        for tt in range(TT):
                            at = (kt % 2) * T + tt * P
                            last = nc.tensor.transpose(bank(4 + b, at, at + P), X[:, tt, kt * P:kt * P + P], ident)
                    last.then_inc(xT_psum, 1)

            pe.wait_ge(x_in, 16)
            pe.wait_ge(consts_in, 16)
            transpose_x(0)
            pe.wait_ge(xT_lo_ready, 4)
            for c in range(3):
                for half in range(2):
                    wide_panel(N_QKV + 2 * c + half, None, half, (2 * c, 2 * c + 1), x_cols)
            pe.wait_ge(v_ready, 2)
            pe.wait_ge(rope_added, 6)
            for b in range(QT // 2):
                for j in (2 * b, 2 * b + 1):
                    for tt in range(TT):
                        at = (j % 2) * T + tt * P
                        last = nc.tensor.transpose(bank(b, at, at + P), roped[:, tt, j, :], ident)
                last.then_inc(qkT_psum, 1)
            pe.wait_ge(qkT_act, 3)
            pe.wait_ge(qkT_dve, 2)

            for s in range(PAIRS + 2):
                if s < PAIRS:
                    if s >= 2:
                        pe.wait_ge(masked, s - 1)
                    for qb in range(TT):
                        for b in range(2):
                            rows = slice(HD * b, HD * b + HD)
                            last = nc.tensor.matmul(bank(2 * (s % 2) + b, qb * T, qb * T + T),
                                                    qkT[rows, s, qb * P:qb * P + P], qkT[rows, PAIRS + s // 4, :],
                                                    start=True, stop=True)
                    last.then_inc(scores, 1)
                if 1 <= s < PAIRS + 1:
                    j = s - 1
                    pe.wait_ge(probs_ready, j + 1)
                    if j:
                        pe.wait_ge(pT_act, j)
                        pe.wait_ge(pT_dve, j)
                    for b in range(2):
                        for kt in range(TT):
                            for qb in range(TT):
                                at = kt * T + qb * P
                                last = nc.tensor.transpose(bank(4 + b, at, at + P),
                                                           probs[:, j % 2, 2 * b + qb, kt * P:kt * P + P], ident)
                    last.then_inc(pT_psum, 1)
                if s >= 2:
                    j = s - 2
                    pe.wait_ge(pT_act, j + 1)
                    pe.wait_ge(pT_dve, j + 1)
                    if j >= 2:
                        pe.wait_ge(o_lo, j - 1)
                    for kt in range(TT):
                        for b in range(2):
                            kv = 2 * (j // 4) + b
                            last = nc.tensor.matmul(psum[HD * b:HD * b + HD, 6 + j % 2, 0:T],
                                                    v[:, kt, kv * HD:kv * HD + HD], pT[:, b, kt, :],
                                                    start=kt == 0, stop=kt == 1)
                    last.then_inc(o_psum, 1)
            pe.wait_ge(o_lo, PAIRS)
            pe.wait_ge(masked, PAIRS)
            for i in range(4):
                tall_panel(N_WO + i, None, ((0, 1), (2, 3)), lambda kk, tt: x_cols(2 * i + kk, tt), i == 0, i == 3)
            transpose_x(1)
            pe.wait_ge(xT_lo_ready, 8)

            def swiglu(first, e, nt, q0, per, gb, ub, yb, lhs, extra=None):
                def q(j, tt):
                    k = q0 + nt * j + tt
                    return k if e is None else e * per + k

                def down(j):
                    pe.wait_ge(hT_lo_ready, q(j, nt - 1) + 1)
                    for half in range(2):
                        def hidden(kk, tt):
                            at = (slice(None), 2 * half + kk, slice(tt * P, tt * P + P))
                            return hT_hi[at], hT_lo[at]
                        tall_panel(first + FFN_AT["down", j, half], e, yb, hidden, j == 0 and half == 0,
                                   j == FB - 1 and half == 1)

                for j in range(FB):
                    if e is not None or j:
                        pe.wait_ge(silu_done, q(j, -1) + 1)
                    for half in range(2):
                        wide_panel(first + FFN_AT["gate", j, half], e, half, gb, lhs)
                    if e is not None or j:
                        pe.wait_ge(hT_lo_ready, q(j, -1) + 1)
                    for half in range(2):
                        wide_panel(first + FFN_AT["up", j, half], e, half, ub, lhs)
                    if j:
                        down(j - 1)
                    if extra:
                        extra(j)
                    for tt in range(nt):
                        pe.wait_ge(h_ready, q(j, tt) + 1)
                        for kk in range(4):
                            last = nc.tensor.transpose(bank(ub[tt], kk * P, kk * P + P), h[:, tt, kk * P:kk * P + P],
                                                       ident)
                        last.then_inc(hT_psum, 1)
                down(FB - 1)

            swiglu(N_FFN, None, TT, 0, 0, G_B, U_B, ((4, 5), (6, 7)), x_cols)

            pe.wait_ge(conv_in, 96)
            pe.wait_ge(pads_zero, 3)
            nc.tensor.transpose(bank(0, 0, 40), conv_rows[:, :], ident[0:40, 0:40])
            for m in range(KT):
                last = nc.tensor.transpose(bank(1, 32 * m, 32 * m + 32), tap_rows[:, m * P:m * P + P],
                                           ident[0:32, 0:32])
            last.then_inc(conv_colsT, 1)
            transpose_x(2)
            pe.wait_ge(xT_lo_ready, 12)
            pe.wait_ge(taps_ready, 2)
            for i in range(4):
                banks = range(0, 4) if i % 2 == 0 else range(4, 8)
                if i == 2:
                    pe.wait_ge(sig_done, 4)
                if i == 3:
                    pe.wait_ge(glu_done, 4)
                for half in range(2):
                    n0 = N_PW1 + 2 * i + half
                    pe.wait_ge(lo_ready, n0 + 1)
                    for m, b in enumerate(banks):
                        for kk in range(4):
                            at = 512 * kk + P * m
                            kt = 4 * half + kk
                            last = three_passes(bank(b, 0, T), panel(n0, at, at + P),
                                                (xT_hi[:, kt, :], xT_lo[:, kt, :]),
                                                half == 0 and kk == 0, half == 1 and kk == 3)
                    last.then_inc(panel_used, 1)
            pe.wait_ge(sig_done, 8)
            pe.wait_ge(glu_done, 8)
            for t, m in enumerate(PE_TILES):
                for i in range(TAP_GROUP):
                    pe.wait_ge(diag_ready, 32 * t + i + 1)
                    nc.tensor.matmul(bank(t, 0, T), diag[:, i, :], glu[:, m, i:i + T], start=i == 0,
                                     stop=False, skip_group_check=True).then_inc(diag_used, 1)
                with pe.Fori(1, 32 // TAP_GROUP) as group:
                    for i in range(TAP_GROUP):
                        pe.wait_ge(diag_ready, group * TAP_GROUP + (32 * t + i + 1))
                        last = nc.tensor.matmul(bank(t, 0, T), diag[:, i, :],
                                                glu[:, m, bass.ds(group * TAP_GROUP + i, T)], start=False,
                                                stop=False, skip_group_check=True)
                        last.then_inc(diag_used, 1)
            pe.wait_ge(conv_dve, TAPS * len(DVE_TILES))
            pe.wait_ge(conv_act, len(PE_TILES))
            for m in range(KT):
                last = nc.tensor.matmul(bank(4, 0, T), mean_w[:, :], cv[:, m, :], start=m == 0, stop=m == KT - 1)
            last.then_inc(mean_psum, 1)
            pe.wait_ge(squared, 1)
            for m in range(KT):
                last = nc.tensor.matmul(bank(5, 0, T), mean_w[:, :], cv_sq[:, m, :], start=m == 0, stop=m == KT - 1)
            last.then_inc(cvar_psum, 1)
            pe.wait_ge(z_lo, 2)
            for i in range(4):
                tall_panel(N_PW2 + i, None, ((0, 1), (2, 3)), lambda kk, tt: x_cols(2 * i + kk, tt), i == 0, i == 3)
            transpose_x(3)
            pe.wait_ge(xT_lo_ready, 16)

            pe.wait_ge(router_in, 16)
            for tt in range(TT):
                for kt in range(KT):
                    for part, s in enumerate(x_cols(kt, tt)):
                        last = nc.tensor.matmul(bank(tt, 0, EXPERTS), s.bitcast(fp32), router[:, kt, :],
                                                start=kt == 0 and part == 0, stop=kt == KT - 1 and part == 1)
            last.then_inc(logits_psum, 1)
            pe.wait_ge(chosen_ready, 1)
            nc.tensor.matmul(bank(2, 0, EXPERTS), tri, chosen[:, 0, :], start=True, stop=True)
            nc.tensor.matmul(bank(3, 0, EXPERTS), ones, chosen[:, 0, :], start=True, stop=False)
            nc.tensor.matmul(bank(3, 0, EXPERTS), tri, chosen[:, 1, :], start=False, stop=True)
            nc.tensor.matmul(bank(4, 0, EXPERTS), ones, chosen[:, 0, :], start=True, stop=False)
            nc.tensor.matmul(bank(4, 0, EXPERTS), ones, chosen[:, 1, :], start=False, stop=True).then_inc(slot_psum, 1)
            pe.wait_ge(routed, 1)

            def gather(turn):
                pe.wait_ge(pick_ready, turn + 1)
                for kt in range(KT):
                    for tt in range(TT):
                        at = (kt % 4) * P
                        last = nc.tensor.matmul(bank(4 + kt // 4, at, at + P), X[:, tt, kt * P:kt * P + P],
                                                pick[:, tt, :], start=tt == 0, stop=tt == 1)
                last.then_inc(xg_psum, 1)

            def scatter(done):
                for tt in range(TT):
                    for k in range(2):
                        last = nc.tensor.matmul(bank(4 + 2 * tt + k), placeT[:, tt * P:tt * P + P],
                                                ye[:, 512 * k:512 * k + 512], start=True, stop=True)
                last.then_inc(done, 1)

            def g_cols(kt, tt):
                return xg_hi[:, kt, :], xg_lo[:, kt, :]

            def experts(p):
                gather(9 * p)
                with pe.Fori(EXPERTS * p, EXPERTS * (p + 1)) as e:
                    pe.wait_ge(xg_lo_ready, e * 2 + (2 + 2 * p))

                    def extra(j):
                        if j == 0:
                            pe.wait_ge(ye_ready, e * 2)
                        if j == 2:
                            pe.wait_ge(placeT_ready, e)
                            scatter(scattered)
                        if j == 3:
                            pe.wait_ge(place_ready, e + 1)
                            pe.wait_ge(y_added, e * 4 + 4)
                            for tt in range(TT):
                                last = nc.tensor.transpose(bank(6, tt * P, tt * P + P), place[:, tt, :], ident)
                            last.then_inc(placeT_psum, 1)
                        if j == FB - 1:
                            gather(e + (1 + p))

                    swiglu(N_MOE, e, 1, TT * FB, FB, EG_B, EU_B, (EY_B,), g_cols, extra)

            pe.wait_ge(moe_zero, 4)
            experts(0)
            again = pe.value_load(overflow[0:1, 0:1], min_val=0, max_val=1)
            with pe.If(again > 0):
                experts(1)
            pe.wait_ge(passes_act, 1)
            pe.wait_ge(passes_dve, 1)
            scatter(last_scatter)


_INS = ['x', 'attn_w_qkv', 'attn_sink', 'attn_w_o', 'conv_pw1_w', 'conv_pw1_b', 'conv_dw_w', 'conv_dw_b',
        'conv_norm_g', 'conv_norm_b', 'conv_pw2_w', 'conv_pw2_b', 'ffn_w_gate', 'ffn_w_up', 'ffn_w_down',
        'moe_router', 'moe_w_gate', 'moe_w_up', 'moe_w_down', 'ln_mix_g', 'ln_mix_b', 'ln_ffn_g', 'ln_ffn_b']


def shape_constants():
    c = np.zeros((P, C_END), np.float32)
    r = np.arange(P)
    c[:, C_ID:C_ID + P] = np.eye(P)
    c[:, C_TRI:C_TRI + P] = r[:, None] < r[None, :]
    c[:, C_ONE:C_ONE + P] = 1.0
    c[:, C_IOTA:C_IOTA + 2 * P] = np.arange(2 * P)[None, :]
    keys = np.arange(T)
    for qb in range(TT):
        far = np.abs(keys[None, :] - (qb * P + r)[:, None]) > 128
        c[:, C_MASK + qb * T:C_MASK + qb * T + T] = np.where(far, np.float32(-1e30), np.float32(0))
    inv_freq = np.float32(10000.0) ** (-np.arange(0, HD, 2, dtype=np.float32) / np.float32(HD))
    for tt in range(TT):
        ang = (tt * P + r).astype(np.float32)[:, None] * inv_freq[None, :]
        c[:, C_COS + tt * 32:C_COS + tt * 32 + 32] = np.cos(ang)
        c[:, C_SIN + tt * 32:C_SIN + tt * 32 + 32] = np.sin(ang)
        c[:, C_NSIN + tt * 32:C_NSIN + tt * 32 + 32] = -np.sin(ang)
    return c


def kernel(**inputs):
    import concourse.bacc as bacc
    from concourse.bass_utils import run_bass_kernel_spmd

    nc = bacc.Bacc("TRN2", target_bir_lowering=False, num_devices=1)
    arrays, args = {}, []
    for name in _INS:
        a = np.ascontiguousarray(inputs[name])
        arrays[f"in_{name}_dram"] = a
        args.append(nc.dram_tensor(f"in_{name}_dram", a.shape, mybir.dt.from_np(a.dtype), kind="ExternalInput").ap())
    c = shape_constants()
    arrays["shape_consts_dram"] = c
    args.append(nc.dram_tensor("shape_consts_dram", c.shape, mybir.dt.float32, kind="ExternalInput").ap())
    args.append(nc.dram_tensor("out_0_dram", (1, T, D), mybir.dt.float32, kind="ExternalOutput").ap())
    build(nc, *args)
    r = run_bass_kernel_spmd(nc, [arrays], core_ids=[0])
    return r.results[0]["out_0_dram"]
```

```python
from contextlib import ExitStack

import concourse.bass as bass
from concourse import mybir
import numpy as np

P = 128
D = 1024
T = 256
TT = T // P
KT = D // P
HEADS, KV, HD = 16, 4, 64
PAIRS = HEADS // 2
QT = PAIRS + KV // 2
TAPS, HALF_TAPS = 31, 15
FF = 3584
FB = FF // 512
EXPERTS = 8
BANK = 512
PANEL = 2048
RAW, SPLIT = 7, 3
PER_FFN = 6 * FB
LN_EPS = 1e-5
ALPHA = 4.0 ** 0.25
DVE_TILES, PE_TILES = (0, 1, 2, 3, 4), (5, 6, 7)
TAP_GROUP = 4

N_QKV = 0
N_WO = N_QKV + 6
N_FFN = N_WO + 4
N_PW1 = N_FFN + PER_FFN
N_PW2 = N_PW1 + 8
N_MOE = N_PW2 + 4

C_ID, C_TRI, C_ONE, C_IOTA = 0, 128, 256, 384
C_MASK = C_IOTA + 256
C_COS = C_MASK + 512
C_SIN = C_COS + TT * 32
C_NSIN = C_SIN + TT * 32
C_END = C_NSIN + TT * 32


def build(nc, x, attn_w_qkv, attn_sink, attn_w_o, conv_pw1_w, conv_pw1_b, conv_dw_w, conv_dw_b,
          conv_norm_g, conv_norm_b, conv_pw2_w, conv_pw2_b, ffn_w_gate, ffn_w_up, ffn_w_down,
          moe_router, moe_w_gate, moe_w_up, moe_w_down, ln_mix_g, ln_mix_b, ln_ffn_g, ln_ffn_b,
          shape_consts, out):
    fp32, f32r = mybir.dt.float32, mybir.dt.float32r
    u32, i32 = mybir.dt.uint32, mybir.dt.int32
    ALU, ACT, AX = mybir.AluOpType, mybir.ActivationFunctionType, mybir.AxisListType
    ctx = ExitStack()

    def sb(name, shape, dt=fp32, where=ctx):
        return where.enter_context(nc.sbuf_tensor(name, shape, dt))

    def sem(name):
        return ctx.enter_context(nc.semaphore(name))

    with ctx:
        raw = sb("raw", [P, RAW, PANEL])
        w_hi = sb("w_hi", [P, SPLIT, PANEL], f32r)
        w_lo = sb("w_lo", [P, SPLIT, PANEL], f32r)
        X = sb("X", [P, TT, D])
        xT_hi = sb("xT_hi", [P, KT, T], f32r)
        xT_lo = sb("xT_lo", [P, KT, T], f32r)
        consts = sb("consts", [P, C_END])
        ln_gb = sb("ln_gb", [P, 2, D])
        stats = sb("stats", [P, TT, 2, 6])
        mean_var = sb("mean_var", [P, TT, 2])
        var_eps = sb("var_eps", [P, TT])
        rstd = sb("rstd", [P, TT])
        minus_half = sb("minus_half", [P, T])
        router = sb("router", [P, KT, EXPERTS])
        psum = ctx.enter_context(nc.psum_tensor("psum", [P, 8, BANK], fp32))
        ident = consts[:, C_ID:C_ID + P]
        ones = consts[:, C_ONE:C_ONE + P]
        tri = consts[:, C_TRI:C_TRI + P]

        attn = ExitStack()
        sink = sb("sink", [P, HEADS], where=attn)
        rope_cos = sb("rope_cos", [P, 2, BANK], where=attn)
        rope_sin = sb("rope_sin", [P, 2, BANK], where=attn)
        roped = sb("roped", [P, TT, QT, P], where=attn)
        qkT = sb("qkT", [P, QT, T], where=attn)
        v = sb("v", [P, TT, KV * HD], where=attn)
        probs = sb("probs", [P, 2, 4, T], where=attn)
        pT = sb("pT", [P, 2, TT, T], where=attn)
        row_max = sb("row_max", [P, 2, 4], where=attn)
        neg_max = sb("neg_max", [P, 2, 4], where=attn)
        sink_arg = sb("sink_arg", [P, 2, 4], where=attn)
        sink_exp = sb("sink_exp", [P, 2, 4], where=attn)
        row_sum = sb("row_sum", [P, 2, 4], where=attn)
        denom = sb("denom", [P, 2, 4], where=attn)
        inv_denom = sb("inv_denom", [P, 2, 4], where=attn)
        attn.close()

        conv = ExitStack()
        conv_rows = sb("conv_rows", [40, P], where=conv)
        tap_rows = sb("tap_rows", [32, D], where=conv)
        conv_cols = sb("conv_cols", [P, 40], where=conv)
        taps = sb("taps", [P, KT, 32], where=conv)
        sig = sb("sig", [P, 4, T], where=conv)
        glu = sb("glu", [P, KT, T + 2 * HALF_TAPS + 2], where=conv)
        cv = sb("cv", [P, KT, T], where=conv)
        cv_sq = sb("cv_sq", [P, KT, T], where=conv)
        cv_var = sb("cv_var", [P, T], where=conv)
        cv_rstd = sb("cv_rstd", [P, T], where=conv)
        diag = sb("diag", [P, TAP_GROUP, P], where=conv)
        pw2_b = sb("pw2_b", [P, D], where=conv)
        mean_w = sb("mean_w", [P, P], where=conv)
        conv.close()

        h_silu = sb("h_silu", [P, TT, BANK])
        h = sb("h", [P, TT, BANK])
        hT_hi = sb("hT_hi", [P, TT, 4, P], f32r)
        hT_lo = sb("hT_lo", [P, TT, 4, P], f32r)
        xg_hi = sb("xg_hi", [P, KT, T], f32r)
        xg_lo = sb("xg_lo", [P, KT, T], f32r)
        ye_hi = sb("ye_hi", [P, TT, D], f32r)
        ye_lo = sb("ye_lo", [P, TT, D], f32r)
        y_acc = sb("y_acc", [P, TT, D])
        pick = sb("pick", [P, TT, T], f32r)
        pickT = sb("pickT", [P, TT, T], f32r)
        logits = sb("logits", [P, TT, EXPERTS])
        top_val = sb("top_val", [P, TT, EXPERTS])
        top_idx = sb("top_idx", [P, TT, EXPERTS], u32)
        top_idx_f = sb("top_idx_f", [P, TT, EXPERTS])
        gate_arg = sb("gate_arg", [P, TT])
        gate_exp = sb("gate_exp", [P, TT])
        gates = sb("gates", [P, TT, 2])
        combine = sb("combine", [P, TT, EXPERTS + 1])
        combine2 = sb("combine2", [P, TT, EXPERTS])
        chosen = sb("chosen", [P, TT, EXPERTS])
        chosen2 = sb("chosen2", [P, TT, EXPERTS])
        slot = sb("slot", [P, TT, EXPERTS + 1])
        two_tiles = sb("two_tiles", [1, EXPERTS], i32)

        landed = [sem(f"landed{i}") for i in range(RAW)]
        hi_ready = sem("hi_ready")
        lo_ready = sem("lo_ready")
        panel_used = sem("panel_used")
        x_in = sem("x_in")
        consts_in = sem("consts_in")
        sink_in = sem("sink_in")
        gb_in = sem("gb_in")
        conv_in = sem("conv_in")
        router_in = sem("router_in")
        out_done = sem("out_done")
        dve_done = sem("dve_done")
        half_set = sem("half_set")
        x_ready = sem("x_ready")
        normed = sem("normed")
        var_ready = sem("var_ready")
        rstd_ready = sem("rstd_ready")
        xT_psum, xT_hi_ready, xT_lo_ready = sem("xT_psum"), sem("xT_hi_ready"), sem("xT_lo_ready")
        rope_terms, rope_added, v_ready = sem("rope_terms"), sem("rope_added"), sem("v_ready")
        qkT_psum, qkT_act, qkT_dve = sem("qkT_psum"), sem("qkT_act"), sem("qkT_dve")
        scores, masked, maxed, exped = sem("scores"), sem("masked"), sem("maxed"), sem("exped")
        inv_ready, probs_ready = sem("inv_ready"), sem("probs_ready")
        pT_psum, pT_act, pT_dve = sem("pT_psum"), sem("pT_act"), sem("pT_dve")
        o_psum, o_hi, o_lo = sem("o_psum"), sem("o_hi"), sem("o_lo")
        silu_done, h_ready = sem("silu_done"), sem("h_ready")
        hT_psum, hT_hi_ready, hT_lo_ready = sem("hT_psum"), sem("hT_hi_ready"), sem("hT_lo_ready")
        pads_zero, conv_colsT, taps_ready = sem("pads_zero"), sem("conv_colsT"), sem("taps_ready")
        sig_done, glu_done = sem("sig_done"), sem("glu_done")
        diag_ready, diag_used = sem("diag_ready"), sem("diag_used")
        conv_act, conv_dve = sem("conv_act"), sem("conv_dve")
        mean_psum, centred, squared, cvar_psum = sem("mean_psum"), sem("centred"), sem("squared"), sem("cvar_psum")
        cvar_ready, crstd_ready, scaled = sem("cvar_ready"), sem("crstd_ready"), sem("scaled")
        act_out, z_hi, z_lo = sem("act_out"), sem("z_hi"), sem("z_lo")
        x_scaled = sem("x_scaled")
        logits_psum, gate_arg_ready, gate_exp_ready = sem("logits_psum"), sem("gate_arg_ready"), sem("gate_exp_ready")
        chosen_ready, slot_psum, routed = sem("chosen_ready"), sem("slot_psum"), sem("routed")
        moe_zero = sem("moe_zero")
        x_hi_ready, x_lo_ready, pick_ready = sem("x_hi_ready"), sem("x_lo_ready"), sem("pick_ready")
        xg_psum, xg_hi_ready, xg_lo_ready = sem("xg_psum"), sem("xg_hi_ready"), sem("xg_lo_ready")
        ye_hi_ready, ye_lo_ready = sem("ye_hi_ready"), sem("ye_lo_ready")
        pickT_psum, pickT_ready = sem("pickT_psum"), sem("pickT_ready")
        scattered, y_added = sem("scattered"), sem("y_added")

        assert PER_FFN % RAW == 0 and PER_FFN % SPLIT == 0
        dmas_before = [0] * (N_MOE + 1)
        seen = [0] * RAW
        for n in range(N_MOE):
            seen[n % RAW] += 2 if N_WO <= n < N_WO + 4 else 1
            dmas_before[n] = seen[n % RAW]

        def number_of(n0, per, e):
            return n0 if e is None else e * per + n0

        def number(n0, e):
            return number_of(n0, PER_FFN, e)

        def landed_at(n0, e):
            if n0 < N_MOE:
                return 16 * dmas_before[n0]
            return number_of(16 * (seen[n0 % RAW] + 1 + (n0 - N_MOE) // RAW), 16 * PER_FFN // RAW, e)

        def wide(w, half, c):
            return w[half * 512:half * 512 + 512, c * 512:c * 512 + 512].rearrange("(k p) n -> p k n", p=P)

        def tall(w, i):
            return w[i * 256:i * 256 + 256, :].rearrange("(k p) n -> p k n", p=P)

        def raw_as(n0, k):
            return raw[:, n0 % RAW, :].rearrange("p (k n) -> p k n", k=k)

        def ffn_panels():
            for j in range(FB):
                for kind in ("gate", "up"):
                    for half in range(2):
                        yield kind, j, half
                if j:
                    for half in range(2):
                        yield "down", j - 1, half
            for half in range(2):
                yield "down", FB - 1, half

        FFN_AT = {what: k for k, what in enumerate(ffn_panels())}

        G_B, U_B, Y_B = (0, 1), (2, 3), ((4, 5), (6, 7))

        def bank(i, a=0, b=BANK):
            return psum[:, i, a:b]

        def heads_view(ap):
            return ap.rearrange("p (h s d) -> p h s d", s=2, d=HD // 2)

        def rope_table(col, tt, n):
            t = consts[:, col + tt * 32:col + tt * 32 + 32]
            return t.unsqueeze(1).unsqueeze(1).broadcast_to([P, n, 2, 32]) if col == C_COS else \
                t.unsqueeze(1).broadcast_to([P, n, 32])

        block = ctx.enter_context(nc.Block())

        @block.sync
        def _(sp):
            def load(n0, e, dst_src):
                if n0 >= RAW:
                    sp.wait_ge(lo_ready, number(n0 - RAW + 1, e))
                for dst, src in dst_src:
                    sp.dma_start(dst, src).then_inc(landed[n0 % RAW], 16)

            def load_ffn(first, e, w_gate, w_up, w_down):
                for k, (kind, j, half) in enumerate(ffn_panels()):
                    if kind == "down":
                        src, dst = tall(w_down, 2 * j + half), raw_as(first + k, 2)
                    else:
                        src, dst = wide(w_gate if kind == "gate" else w_up, half, j), raw_as(first + k, 4)
                    load(first + k, e, [(dst, src)])

            sp.dma_start(X[:, :, :], x[0].rearrange("(t p) d -> p t d", p=P)).then_inc(x_in, 16)
            sp.dma_start(consts[:, :], shape_consts).then_inc(consts_in, 16)
            for c in range(3):
                for half in range(2):
                    n = N_QKV + 2 * c + half
                    load(n, None, [(raw_as(n, 4), wide(attn_w_qkv[0], half, c))])
            wo = attn_w_o[0].rearrange("(kv g d) n -> kv d g n", kv=KV, d=HD)
            for i in range(4):
                n = N_WO + i
                load(n, None, [(raw_as(n, 2)[HD * b:HD * b + HD], wo[2 * (i // 2) + b][:, 2 * (i % 2):2 * (i % 2) + 2, :])
                               for b in range(2)])
            load_ffn(N_FFN, None, ffn_w_gate[0], ffn_w_up[0], ffn_w_down[0])
            for i, c in enumerate((2, 0, 3, 1)):
                for half in range(2):
                    n = N_PW1 + 2 * i + half
                    load(n, None, [(raw_as(n, 4), wide(conv_pw1_w[0], half, c))])
            for i in range(4):
                load(N_PW2 + i, None, [(raw_as(N_PW2 + i, 2), tall(conv_pw2_w[0], i))])

            with sp.Fori(0, EXPERTS) as e:
                load_ffn(N_MOE, e, moe_w_gate[0, bass.ds(e, 1)][0], moe_w_up[0, bass.ds(e, 1)][0],
                         moe_w_down[0, bass.ds(e, 1)][0])
            for k in range(2):
                load(N_MOE + k, EXPERTS, [(raw_as(N_MOE + k, 4), wide(moe_w_gate[0, 0], k, 0))])
            sp.wait_ge(x_ready, 16)
            sp.dma_start(out[0].rearrange("(t p) d -> p t d", p=P), X[:, :, :]).then_inc(out_done, 16)
            sp.wait_ge(out_done, 16)

        @block.gpsimd
        def _(pool):
            pool.dma_start(sink[:, :], attn_sink[0].partition_broadcast(P)).then_inc(sink_in, 16)

            def load_norm(i, g, b):
                if i:
                    pool.wait_ge(x_ready, 4 * i)
                pool.dma_start(ln_gb[:, 0, :], g.partition_broadcast(P)).then_inc(gb_in, 16)
                pool.dma_start(ln_gb[:, 1, :], b.partition_broadcast(P)).then_inc(gb_in, 16)

            load_norm(0, ln_mix_g[0], ln_mix_b[0])
            nc.gpsimd.memset(minus_half[:, :], -0.5).then_inc(half_set, 1)

            for c in range(3):
                for tt in range(TT):
                    i = 2 * c + tt
                    pool.wait_ge(rope_terms, i + 1)
                    n = 4 if c == 2 else 8
                    a, b = rope_cos[:, i % 2, 0:n * HD], rope_sin[:, i % 2, 0:n * HD]
                    if c == 2:
                        o = roped[:, tt, PAIRS:QT, :].rearrange("p a n -> p (a n)")
                    else:
                        a = a.rearrange("p (b g d) -> p b g d", b=2, d=HD)
                        b = b.rearrange("p (b g d) -> p b g d", b=2, d=HD)
                        o = roped[:, tt, 4 * c:4 * c + 4, :].rearrange("p g (b d) -> p b g d", b=2)
                    nc.gpsimd.tensor_tensor(o, a, b, ALU.add).then_inc(rope_added, 1)

            for j in range(PAIRS):
                pool.wait_ge(inv_ready, j + 1)
                for i in range(4):
                    last = nc.gpsimd.tensor_scalar(probs[:, j % 2, i, :], probs[:, j % 2, i, :],
                                                   inv_denom[:, j % 2, i:i + 1], None, ALU.mult)
                last.then_inc(probs_ready, 1)

            def norm_tail(i):
                pool.wait_ge(half_set, 1)
                for tt in range(TT):
                    pool.wait_ge(var_ready, 2 * i + tt + 1)
                    nc.gpsimd.tensor_tensor(rstd[:, tt:tt + 1], var_eps[:, tt:tt + 1],
                                            minus_half[:, tt:tt + 1], ALU.pow).then_inc(rstd_ready, 1)
                pool.wait_ge(gb_in, 32 * (i + 1))
                for half in range(2):
                    for tt in range(TT):
                        s = slice(512 * half, 512 * half + 512)
                        pool.wait_ge(normed, 4 * i + 2 * half + tt + 1)
                        nc.gpsimd.tensor_tensor(X[:, tt, s], X[:, tt, s], ln_gb[:, 1, s], ALU.add).then_inc(x_ready, 1)

            norm_tail(0)
            load_norm(1, ln_ffn_g[0], ln_ffn_b[0])
            norm_tail(1)
            load_norm(2, ln_mix_g[1], ln_mix_b[1])
            nc.gpsimd.memset(glu[:, :, :], 0.0).then_inc(pads_zero, 1)
            nc.gpsimd.memset(tap_rows[:, :], 0.0).then_inc(pads_zero, 1)
            nc.gpsimd.memset(mean_w[:, :], 1.0 / D).then_inc(pads_zero, 1)
            pool.wait_ge(pads_zero, 2)
            pool.dma_start(tap_rows[0:TAPS, :], conv_dw_w[0]).then_inc(conv_in, 16)
            for at, vec in ((0, conv_pw1_b), (16, conv_dw_b), (24, conv_norm_g), (32, conv_norm_b)):
                rows = vec.shape[1] // P
                pool.dma_start(conv_rows[at:at + rows, :], vec[0].rearrange("(r c) -> r c", c=P)).then_inc(conv_in, 16)
            pool.dma_start(pw2_b[:, :], conv_pw2_b[0].partition_broadcast(P)).then_inc(conv_in, 16)
            pool.dma_start(router[:, :, :], moe_router[0].rearrange("(k p) e -> p k e", p=P)).then_inc(router_in, 16)
            pool.wait_ge(xT_psum, 12)
            nc.gpsimd.tensor_scalar(X[:, :, :], X[:, :, :], ALPHA, None, ALU.mult).then_inc(x_scaled, 1)
            pool.wait_ge(x_scaled, 1)
            pool.wait_ge(conv_in, 96)
            for tt in range(TT):
                nc.gpsimd.tensor_tensor(X[:, tt, :], X[:, tt, :], pw2_b[:, :], ALU.add).then_inc(x_scaled, 1)
            pool.wait_ge(cvar_ready, 1)
            nc.gpsimd.tensor_tensor(cv_rstd[:, :], cv_var[:, :], minus_half[:, :], ALU.pow).then_inc(crstd_ready, 1)
            norm_tail(2)
            load_norm(3, ln_ffn_g[1], ln_ffn_b[1])
            nc.gpsimd.memset(y_acc[:, :, :], 0.0).then_inc(y_added, 1)
            nc.gpsimd.memset(ye_hi[:, :, :].bitcast(fp32), 0.0).then_inc(ye_hi_ready, 1)
            nc.gpsimd.memset(ye_lo[:, :, :].bitcast(fp32), 0.0).then_inc(ye_lo_ready, 1)
            nc.gpsimd.memset(pickT[:, :, :].bitcast(fp32), 0.0).then_inc(pickT_ready, 1)
            nc.gpsimd.memset(slot[:, :, :], -1.0).then_inc(moe_zero, 1)
            nc.gpsimd.memset(combine[:, :, :], 0.0).then_inc(moe_zero, 1)
            norm_tail(3)

        @block.scalar
        def _(act):
            def round_panel(n0, e=None):
                act.wait_ge(landed[n0 % RAW], landed_at(n0, e))
                if n0 >= SPLIT:
                    act.wait_ge(panel_used, number(n0 - SPLIT + 1, e))
                nc.scalar.activation(w_hi[:, n0 % SPLIT, :], raw[:, n0 % RAW, :], ACT.Copy).then_inc(hi_ready, 1)

            def round_xT(r):
                for b in range(4):
                    act.wait_ge(xT_psum, 4 * r + b + 1)
                    nc.scalar.activation(xT_hi[:, 2 * b:2 * b + 2, :].rearrange("p k t -> p (k t)"), bank(4 + b),
                                         ACT.Copy).then_inc(xT_hi_ready, 1)

            round_panel(0)
            round_xT(0)
            for n in range(1, 6):
                round_panel(n)
            for tt in range(TT):
                act.wait_ge(rope_terms, 5 + tt)
                nc.scalar.activation(v[:, tt, :], bank(4 + tt, 256), ACT.Copy).then_inc(v_ready, 1)
            for b in (0, 2, 4):
                act.wait_ge(qkT_psum, b + 1)
                nc.scalar.activation(qkT[:, 2 * b:2 * b + 2, :].rearrange("p k t -> p (k t)"), bank(b),
                                     ACT.Copy).then_inc(qkT_act, 1)

            for s in range(PAIRS + 2):
                if s < PAIRS:
                    act.wait_ge(maxed, s + 1)
                    if s >= 2:
                        act.wait_ge(inv_ready, s - 1)
                    for i in range(4):
                        nc.scalar.activation(probs[:, s % 2, i, :], probs[:, s % 2, i, :], ACT.Exp,
                                             bias=neg_max[:, s % 2, i:i + 1], accum_out=row_sum[:, s % 2, i:i + 1])
                    nc.scalar.activation(sink_exp[:, s % 2, :], sink_arg[:, s % 2, :], ACT.Exp).then_inc(exped, 1)
                if 1 <= s < PAIRS + 1:
                    act.wait_ge(pT_psum, s)
                    if s >= 2:
                        act.wait_ge(o_psum, s - 1)
                    nc.scalar.activation(pT[:, 0, :, :].rearrange("p k t -> p (k t)"), bank(4),
                                         ACT.Copy).then_inc(pT_act, 1)
                if s >= 2:
                    j = s - 2
                    act.wait_ge(o_psum, j + 1)
                    nc.scalar.activation(xT_hi[:, j, :], bank(6 + j % 2, 0, T), ACT.Copy).then_inc(o_hi, 1)

            for n in range(N_WO, N_WO + 4):
                round_panel(n)
            round_panel(N_FFN)
            round_xT(1)

            def swiglu(first, e, nt, q0):
                def q(j):
                    return number_of(q0 + j, FB, e)

                def panel(kind, j, half):
                    if e is None and kind == "gate" and j == 0 and half == 0:
                        return
                    round_panel(first + FFN_AT[kind, j, half], e)

                def round_hT(j):
                    act.wait_ge(hT_psum, q(j) + 1)
                    nc.scalar.activation(hT_hi[:, 0:nt].rearrange("p t k n -> p t (k n)"), psum[:, 2:2 + nt, :],
                                         ACT.Copy).then_inc(hT_hi_ready, 1)

                for j in range(FB):
                    if j or e is None:
                        panel("gate", j, 0)
                        panel("gate", j, 1)
                    if j:
                        round_hT(j - 1)
                    panel("up", j, 0)
                    panel("up", j, 1)
                    act.wait_ge(panel_used, number(first + FFN_AT["gate", j, 1] + 1, e))
                    if e is not None or j:
                        act.wait_ge(h_ready, q(j))
                    nc.scalar.activation(h_silu[:, 0:nt, :], psum[:, 0:nt, :], ACT.Silu).then_inc(silu_done, 1)
                    if e is not None and j == 1:
                        act.wait_ge(pickT_psum, e + 1)
                        nc.scalar.activation(pickT[:, :, :].rearrange("p s t -> p (s t)"), bank(4),
                                             ACT.Copy).then_inc(pickT_ready, 1)
                    if j:
                        panel("down", j - 1, 0)
                        panel("down", j - 1, 1)
                if e is not None:
                    copy_gathered(e + 1, 0)
                panel("down", FB - 1, 0)
                panel("down", FB - 1, 1)
                round_hT(FB - 1)
                if e is not None:
                    copy_gathered(e + 1, 1)
                    round_panel(first + PER_FFN, e)
                    copy_gathered(e + 1, 2)
                    round_panel(first + PER_FFN + 1, e)
                    copy_gathered(e + 1, 3)
                    act.wait_ge(panel_used, number(first + PER_FFN, e))
                    nc.scalar.activation(ye_hi[:, 0:nt, :].rearrange("p s (k n) -> p (s k) n", k=2),
                                         psum[:, 4:4 + 2 * nt, :], ACT.Copy).then_inc(ye_hi_ready, 1)

            def copy_gathered(turn, i):
                act.wait_ge(xg_psum, turn * 4 + (i + 1))
                nc.scalar.activation(xg_hi[:, 2 * i:2 * i + 2, :].rearrange("p k t -> p (k t)"), bank(0),
                                     ACT.Copy).then_inc(xg_hi_ready, 1)

            swiglu(N_FFN, None, TT, 0)
            round_panel(N_PW1)
            act.wait_ge(conv_colsT, 1)
            nc.scalar.activation(conv_cols[:, :], bank(0, 0, 40), ACT.Copy).then_inc(taps_ready, 1)
            nc.scalar.activation(taps[:, :, :].rearrange("p k t -> p (k t)"), bank(1, 0, KT * 32),
                                 ACT.Copy).then_inc(taps_ready, 1)
            round_xT(2)
            act.wait_ge(taps_ready, 2)
            for n in range(N_PW1 + 1, N_PW1 + 8):
                round_panel(n)
                if n in (N_PW1 + 2, N_PW1 + 6):
                    c = (n - N_PW1) // 4
                    act.wait_ge(panel_used, n)
                    if c:
                        act.wait_ge(glu_done, 4)
                    for m in range(4):
                        col = 8 + 4 * c + m
                        nc.scalar.activation(sig[:, m, :], bank(m, 0, T), ACT.Sigmoid,
                                             bias=conv_cols[:, col:col + 1]).then_inc(sig_done, 1)
            for t, m in enumerate(PE_TILES):
                def diagonal(i, tap, group):
                    if t or group is not None:
                        before = (32 * t if group is None else group * TAP_GROUP + 32 * t) + i + 1 - TAP_GROUP
                        act.wait_ge(diag_used, before)
                    nc.scalar.activation(diag[:, i, :], ident, ACT.Copy, scale=tap).then_inc(diag_ready, 1)

                for i in range(TAP_GROUP):
                    diagonal(i, taps[:, m, i:i + 1], None)
                with act.Fori(1, 32 // TAP_GROUP) as group:
                    for i in range(TAP_GROUP):
                        diagonal(i, taps[:, m, bass.ds(group * TAP_GROUP + i, 1)], group)
            for t, m in enumerate(PE_TILES):
                act.wait_ge(diag_used, 32 * (t + 1))
                nc.scalar.activation(cv[:, m, :], bank(t, 0, T), ACT.Identity,
                                     bias=conv_cols[:, 16 + m:17 + m]).then_inc(conv_act, 1)
            act.wait_ge(centred, 1)
            nc.scalar.activation(cv_sq[:, :, :], cv[:, :, :], ACT.Square).then_inc(squared, 1)
            act.wait_ge(scaled, 1)
            for m in range(KT):
                nc.scalar.activation(cv_sq[:, m, :], cv[:, m, :], ACT.Silu, scale=conv_cols[:, 24 + m:25 + m],
                                     bias=conv_cols[:, 32 + m:33 + m]).then_inc(act_out, 1)
            for i in range(2):
                act.wait_ge(act_out, 4 * i + 4)
                nc.scalar.activation(xT_hi[:, 4 * i:4 * i + 4, :], cv_sq[:, 4 * i:4 * i + 4, :], ACT.Copy).then_inc(z_hi, 1)
            for n in range(N_PW2, N_PW2 + 4):
                round_panel(n)
            round_xT(3)
            act.wait_ge(gate_arg_ready, 1)
            nc.scalar.activation(gate_exp[:, :], gate_arg[:, :], ACT.Exp).then_inc(gate_exp_ready, 1)

            act.wait_ge(logits_psum, 1)
            nc.scalar.activation(xT_hi[:, :, :].rearrange("p k t -> p (k t)"), X[:, :, :].rearrange("p t d -> p (t d)"),
                                 ACT.Copy).then_inc(x_hi_ready, 1)
            act.wait_ge(moe_zero, 2)
            for i in range(4):
                copy_gathered(0, i)
            round_panel(N_MOE)
            round_panel(N_MOE + 1)
            act.wait_ge(routed, 1)
            with act.Fori(0, EXPERTS) as e:
                both_tiles = act.value_load(two_tiles[0:1, bass.ds(e, 1)], min_val=0, max_val=1)
                with act.If(both_tiles > 0):
                    swiglu(N_MOE, e, TT, FB)
                with act.Else():
                    swiglu(N_MOE, e, 1, FB)

        @block.vector
        def _(dve):
            steps = [0]

            def step(ins):
                steps[0] += 1
                ins.then_inc(dve_done, 1)
                dve.wait_ge(dve_done, steps[0])

            def rest_panel(n0, e=None):
                dve.wait_ge(hi_ready, number(n0 + 1, e))
                if n0 >= SPLIT:
                    dve.wait_ge(panel_used, number(n0 - SPLIT + 1, e))
                nc.vector.tensor_tensor(w_lo[:, n0 % SPLIT, :], raw[:, n0 % RAW, :],
                                        w_hi[:, n0 % SPLIT, :].bitcast(fp32), ALU.subtract).then_inc(lo_ready, 1)

            def rest_xT(r):
                for b in range(4):
                    dve.wait_ge(xT_hi_ready, 4 * r + b + 1)
                    d = slice(2 * b, 2 * b + 2)
                    nc.vector.tensor_tensor(xT_lo[:, d, :].rearrange("p k t -> p (k t)"), bank(4 + b),
                                            xT_hi[:, d, :].rearrange("p k t -> p (k t)").bitcast(fp32),
                                            ALU.subtract).then_inc(xT_lo_ready, 1)

            rest_panel(0)
            rest_xT(0)
            for n in range(1, 6):
                rest_panel(n)
            dve.wait_ge(consts_in, 16)
            for c in range(3):
                dve.wait_ge(panel_used, 2 * c + 2)
                for tt in range(TT):
                    i = 2 * c + tt
                    n = 4 if c == 2 else 8
                    src = heads_view(bank(2 * c + tt, 0, n * HD))
                    if i >= 2:
                        dve.wait_ge(rope_added, i - 1)
                    nc.vector.tensor_tensor(heads_view(rope_cos[:, i % 2, 0:n * HD]), src,
                                            rope_table(C_COS, tt, n), ALU.mult)
                    dst = heads_view(rope_sin[:, i % 2, 0:n * HD])
                    nc.vector.tensor_tensor(dst[:, :, 0, :], src[:, :, 1, :], rope_table(C_NSIN, tt, n), ALU.mult)
                    nc.vector.tensor_tensor(dst[:, :, 1, :], src[:, :, 0, :], rope_table(C_SIN, tt, n),
                                            ALU.mult).then_inc(rope_terms, 1)
            for b in (1, 3):
                dve.wait_ge(qkT_psum, b + 1)
                nc.vector.tensor_copy(qkT[:, 2 * b:2 * b + 2, :].rearrange("p k t -> p (k t)"),
                                      bank(b)).then_inc(qkT_dve, 1)
            dve.wait_ge(sink_in, 16)
            mask = consts[:, C_MASK:C_MASK + 512].unsqueeze(1).broadcast_to([P, 2, 512])
            for s in range(PAIRS + 2):
                if s < PAIRS:
                    k = s % 2
                    dve.wait_ge(scores, s + 1)
                    if s >= 2:
                        dve.wait_ge(pT_psum, s - 1)
                    nc.vector.scalar_tensor_tensor(
                        probs[:, k, :, :].rearrange("p (b q) t -> p b (q t)", b=2), psum[:, 2 * k:2 * k + 2, :],
                        HD ** -0.5, mask, ALU.mult, ALU.add).then_inc(masked, 1)
                    dve.wait_ge(masked, s + 1)
                    step(nc.vector.reduce_max(row_max[:, k, :], probs[:, k, :, :], AX.X))
                    first = (2 * (s // 4)) * 4 + s % 4
                    sinks = sink[:, first:first + 5:4].unsqueeze(2).broadcast_to([P, 2, 2])
                    by_head = lambda t: t[:, k, :].rearrange("p (b q) -> p b q", b=2)
                    step(nc.vector.tensor_tensor(by_head(row_max), by_head(row_max), sinks, ALU.max))
                    step(nc.vector.tensor_scalar(neg_max[:, k, :], row_max[:, k, :], -1.0, None, ALU.mult))
                    nc.vector.tensor_tensor(by_head(sink_arg), by_head(neg_max), sinks, ALU.add).then_inc(maxed, 1)
                if 1 <= s < PAIRS + 1:
                    dve.wait_ge(pT_psum, s)
                    if s >= 2:
                        dve.wait_ge(o_psum, s - 1)
                    nc.vector.tensor_copy(pT[:, 1, :, :].rearrange("p k t -> p (k t)"), bank(5)).then_inc(pT_dve, 1)
                if s < PAIRS:
                    dve.wait_ge(exped, s + 1)
                    step(nc.vector.tensor_tensor(denom[:, k, :], row_sum[:, k, :], sink_exp[:, k, :], ALU.add))
                    if s >= 2:
                        dve.wait_ge(probs_ready, s - 1)
                    nc.vector.reciprocal(inv_denom[:, k, :], denom[:, k, :]).then_inc(inv_ready, 1)
                if s >= 2:
                    j = s - 2
                    dve.wait_ge(o_hi, j + 1)
                    nc.vector.tensor_tensor(xT_lo[:, j, :], bank(6 + j % 2, 0, T), xT_hi[:, j, :].bitcast(fp32),
                                            ALU.subtract).then_inc(o_lo, 1)
            for n in range(N_WO, N_WO + 4):
                rest_panel(n)
            rest_panel(N_FFN)

            def layer_norm(i, mix, alpha):
                halves = [slice(512 * k, 512 * k + 512) for k in range(2)]
                for tt in range(TT):
                    for k, s in enumerate(halves):
                        step(nc.vector.scalar_tensor_tensor(X[:, tt, s], X[:, tt, s], alpha, mix(tt, k),
                                                            ALU.mult, ALU.add))
                        nc.vector.bn_stats(stats[:, tt, k, :], X[:, tt, s]).then_inc(dve_done, 1)
                        steps[0] += 1
                    dve.wait_ge(dve_done, steps[0])
                    step(nc.vector.bn_aggr(mean_var[:, tt, :], stats[:, tt, :, :].rearrange("p k s -> p (k s)")))
                    nc.vector.tensor_scalar(var_eps[:, tt:tt + 1], mean_var[:, tt, 1:2], LN_EPS, None,
                                            ALU.add).then_inc(var_ready, 1)
                for tt in range(TT):
                    dve.wait_ge(rstd_ready, 2 * i + tt + 1)
                    step(nc.vector.tensor_scalar(X[:, tt, :], X[:, tt, :], mean_var[:, tt, 0:1], rstd[:, tt:tt + 1],
                                                 ALU.subtract, ALU.mult))
                dve.wait_ge(gb_in, 32 * (i + 1))
                for s in halves:
                    for tt in range(TT):
                        nc.vector.tensor_tensor(X[:, tt, s], X[:, tt, s], ln_gb[:, 0, s], ALU.mult).then_inc(normed, 1)

            dve.wait_ge(panel_used, N_WO + 4)
            layer_norm(0, lambda tt, k: bank(2 * tt + k), ALPHA)
            rest_xT(1)

            def swiglu(first, e, nt, q0):
                def q(j):
                    return number_of(q0 + j, FB, e)

                def panel(kind, j, half):
                    if e is None and kind == "gate" and j == 0 and half == 0:
                        return
                    rest_panel(first + FFN_AT[kind, j, half], e)

                def rest_hT(j):
                    dve.wait_ge(hT_hi_ready, q(j) + 1)
                    flat = lambda t: t[:, 0:nt].rearrange("p t k n -> p t (k n)")
                    nc.vector.tensor_tensor(flat(hT_lo), psum[:, 2:2 + nt, :], flat(hT_hi).bitcast(fp32),
                                            ALU.subtract).then_inc(hT_lo_ready, 1)

                for j in range(FB):
                    if j or e is None:
                        panel("gate", j, 0)
                        panel("gate", j, 1)
                    if j:
                        rest_hT(j - 1)
                    if e is not None and j == 1:
                        add_scattered(e)
                    panel("up", j, 0)
                    panel("up", j, 1)
                    if e is not None and j == 2:
                        dve.wait_ge(pickT_psum, e + 1)
                        one_hot(bass.ds(e + 1, 1))
                    if j:
                        panel("down", j - 1, 0)
                        panel("down", j - 1, 1)
                    dve.wait_ge(panel_used, number(first + FFN_AT["up", j, 1] + 1, e))
                    dve.wait_ge(silu_done, q(j) + 1)
                    if e is not None or j:
                        dve.wait_ge(hT_psum, q(j))
                    nc.vector.tensor_tensor(h[:, 0:nt, :], h_silu[:, 0:nt, :], psum[:, 2:2 + nt, :],
                                            ALU.mult).then_inc(h_ready, 1)
                if e is not None:
                    copy_gathered(e + 1, 0)
                panel("down", FB - 1, 0)
                panel("down", FB - 1, 1)
                rest_hT(FB - 1)
                if e is not None:
                    copy_gathered(e + 1, 1)
                    rest_panel(first + PER_FFN, e)
                    copy_gathered(e + 1, 2)
                    rest_panel(first + PER_FFN + 1, e)
                    copy_gathered(e + 1, 3)
                    dve.wait_ge(ye_hi_ready, e + 2)
                    rows = lambda t: t[:, 0:nt, :].rearrange("p s (k n) -> p (s k) n", k=2)
                    nc.vector.tensor_tensor(rows(ye_lo), psum[:, 4:4 + 2 * nt, :], rows(ye_hi).bitcast(fp32),
                                            ALU.subtract).then_inc(ye_lo_ready, 1)

            def copy_gathered(turn, i):
                dve.wait_ge(xg_psum, turn * 4 + (i + 1))
                nc.vector.tensor_copy(xg_lo[:, 2 * i:2 * i + 2, :].rearrange("p k t -> p (k t)"),
                                      bank(1)).then_inc(xg_lo_ready, 1)

            def one_hot(e):
                for tt in range(TT):
                    last = nc.vector.tensor_scalar(pick[:, tt, :], consts[:, C_IOTA:C_IOTA + T], slot[:, tt, e], None,
                                                   ALU.is_equal)
                last.then_inc(pick_ready, 1)

            def add_scattered(e):
                dve.wait_ge(scattered, e + 1)
                for tt in range(TT):
                    for k in range(2):
                        s = slice(512 * k, 512 * k + 512)
                        gate = combine[:, tt, e:e + 1] if e is EXPERTS else combine[:, tt, bass.ds(e, 1)]
                        dve.wait_ge(y_added, e * 4 + 1)
                        nc.vector.scalar_tensor_tensor(y_acc[:, tt, s], bank(4 + 2 * tt + k), gate, y_acc[:, tt, s],
                                                       ALU.mult, ALU.add).then_inc(y_added, 1)

            swiglu(N_FFN, None, TT, 0)
            rest_panel(N_PW1)
            dve.wait_ge(panel_used, N_FFN + PER_FFN)
            layer_norm(1, lambda tt, k: bank(4 + 2 * tt + k), ALPHA)
            rest_xT(2)
            dve.wait_ge(taps_ready, 2)
            dve.wait_ge(pads_zero, 3)

            def gated(c):
                dve.wait_ge(panel_used, N_PW1 + 4 * c + 4)
                for m in range(4):
                    col = 4 * c + m
                    dve.wait_ge(sig_done, col + 1)
                    nc.vector.scalar_tensor_tensor(glu[:, col, HALF_TAPS:HALF_TAPS + T], bank(4 + m, 0, T),
                                                   conv_cols[:, col:col + 1], sig[:, m, :], ALU.add,
                                                   ALU.mult).then_inc(glu_done, 1)

            def convolve(tiles, done):
                for m in tiles:
                    nc.vector.tensor_scalar(cv[:, m, :], glu[:, m, 0:T], taps[:, m, 0:1], conv_cols[:, 16 + m:17 + m],
                                            ALU.mult, ALU.add).then_inc(conv_dve, 1)
                with dve.Fori(1, TAPS) as tap:
                    for i, m in enumerate(tiles):
                        dve.wait_ge(conv_dve, tap * len(tiles) + (done + i + 1 - len(tiles)))
                        nc.vector.scalar_tensor_tensor(cv[:, m, :], glu[:, m, bass.ds(tap, T)],
                                                       taps[:, m, bass.ds(tap, 1)], cv[:, m, :], ALU.mult,
                                                       ALU.add).then_inc(conv_dve, 1)

            for n in range(N_PW1 + 1, N_PW1 + 5):
                rest_panel(n)
            gated(0)
            for n in range(N_PW1 + 5, N_PW1 + 8):
                rest_panel(n)
            dve.wait_ge(glu_done, 4)
            gated(1)
            dve.wait_ge(glu_done, 8)
            convolve(DVE_TILES[:4], 0)
            convolve(DVE_TILES[4:], 4 * TAPS)
            dve.wait_ge(mean_psum, 1)
            nc.vector.tensor_tensor(cv[:, :, :], cv[:, :, :], bank(4, 0, T).unsqueeze(1).broadcast_to([P, KT, T]),
                                    ALU.subtract).then_inc(centred, 1)
            dve.wait_ge(cvar_psum, 1)
            nc.vector.tensor_scalar(cv_var[:, :], bank(5, 0, T), LN_EPS, None, ALU.add).then_inc(cvar_ready, 1)
            dve.wait_ge(crstd_ready, 1)
            nc.vector.tensor_tensor(cv[:, :, :], cv[:, :, :], cv_rstd[:, :].unsqueeze(1).broadcast_to([P, KT, T]),
                                    ALU.mult).then_inc(scaled, 1)
            for i in range(2):
                dve.wait_ge(z_hi, i + 1)
                nc.vector.tensor_tensor(xT_lo[:, 4 * i:4 * i + 4, :], cv_sq[:, 4 * i:4 * i + 4, :],
                                        xT_hi[:, 4 * i:4 * i + 4, :].bitcast(fp32), ALU.subtract).then_inc(z_lo, 1)
            for n in range(N_PW2, N_PW2 + 4):
                rest_panel(n)
            dve.wait_ge(panel_used, N_PW2 + 4)
            dve.wait_ge(x_scaled, 3)
            layer_norm(2, lambda tt, k: bank(2 * tt + k), 1.0)
            rest_xT(3)

            dve.wait_ge(logits_psum, 1)
            for tt in range(TT):
                step(nc.vector.tensor_copy(logits[:, tt, :], bank(tt, 0, EXPERTS)))
                step(nc.vector.max(top_val[:, tt, :], logits[:, tt, :]))
                step(nc.vector.max_index(top_idx[:, tt, :], top_val[:, tt, :], logits[:, tt, :]))
            step(nc.vector.tensor_copy(top_idx_f[:, :, :], top_idx[:, :, :]))
            nc.vector.tensor_tensor(gate_arg[:, :], top_val[:, :, 1], top_val[:, :, 0],
                                    ALU.subtract).then_inc(gate_arg_ready, 1)
            iota8 = consts[:, C_IOTA:C_IOTA + EXPERTS]
            for tt in range(TT):
                step(nc.vector.tensor_scalar(chosen2[:, tt, :], iota8, top_idx_f[:, tt, 1:2], None, ALU.is_equal))
                step(nc.vector.scalar_tensor_tensor(chosen[:, tt, :], iota8, top_idx_f[:, tt, 0:1], chosen2[:, tt, :],
                                                    ALU.is_equal, ALU.add))
            dve.wait_ge(moe_zero, 2)
            nc.vector.memset(combine[:, :, 0:1], 0.0).then_inc(chosen_ready, 1)
            dve.wait_ge(gate_exp_ready, 1)
            step(nc.vector.tensor_scalar(gate_arg[:, :], gate_exp[:, :], 1.0, None, ALU.add))
            step(nc.vector.reciprocal(gates[:, :, 0], gate_arg[:, :]))
            step(nc.vector.tensor_tensor(gates[:, :, 1], gates[:, :, 0], gate_exp[:, :], ALU.mult))
            for tt in range(TT):
                step(nc.vector.tensor_scalar(combine[:, tt, 1:], iota8, top_idx_f[:, tt, 0:1], gates[:, tt, 0:1],
                                             ALU.is_equal, ALU.mult))
                step(nc.vector.tensor_scalar(combine2[:, tt, :], iota8, top_idx_f[:, tt, 1:2], gates[:, tt, 1:2],
                                             ALU.is_equal, ALU.mult))
            step(nc.vector.tensor_tensor(combine[:, :, 1:], combine[:, :, 1:], combine2[:, :, :], ALU.add))
            dve.wait_ge(slot_psum, 1)
            for tt in range(TT):
                step(nc.vector.scalar_tensor_tensor(slot[:, tt, 0:EXPERTS], bank(2 + tt, 0, EXPERTS), 1.0,
                                                    chosen[:, tt, :], ALU.add, ALU.mult))
            step(nc.vector.tensor_scalar(slot[:, :, 0:EXPERTS], slot[:, :, 0:EXPERTS], -1.0, None, ALU.add))
            nc.vector.tensor_scalar(two_tiles[0:1, :], psum[0:1, 4, 0:EXPERTS], P + 0.5, None,
                                    ALU.is_gt).then_inc(routed, 1)
            one_hot(slice(0, 1))
            dve.wait_ge(x_hi_ready, 1)
            nc.vector.tensor_tensor(xT_lo[:, :, :].rearrange("p k t -> p (k t)"),
                                    X[:, :, :].rearrange("p t d -> p (t d)"),
                                    xT_hi[:, :, :].rearrange("p k t -> p (k t)").bitcast(fp32),
                                    ALU.subtract).then_inc(x_lo_ready, 1)
            for i in range(4):
                copy_gathered(0, i)
            rest_panel(N_MOE)
            rest_panel(N_MOE + 1)
            dve.wait_ge(routed, 1)
            with dve.Fori(0, EXPERTS) as e:
                both_tiles = dve.value_load(two_tiles[0:1, bass.ds(e, 1)], min_val=0, max_val=1)
                with dve.If(both_tiles > 0):
                    swiglu(N_MOE, e, TT, FB)
                with dve.Else():
                    swiglu(N_MOE, e, 1, FB)
            add_scattered(EXPERTS)
            dve.wait_ge(y_added, 4 * (EXPERTS + 1) + 1)
            layer_norm(3, lambda tt, k: y_acc[:, tt, 512 * k:512 * k + 512], ALPHA)

        @block.tensor
        def _(pe):
            def three_passes(o, st, mv, start, stop):
                nc.tensor.matmul(o, st[0], mv[0], start=start, stop=False)
                nc.tensor.matmul(o, st[0], mv[1], start=False, stop=False)
                return nc.tensor.matmul(o, st[1], mv[0], start=False, stop=stop)

            def both(hi, lo, *at):
                return hi[at], lo[at]

            def panel(n0, a, b):
                return w_hi[:, n0 % SPLIT, a:b], w_lo[:, n0 % SPLIT, a:b]

            def wide_panel(n0, e, half, banks, lhs):
                pe.wait_ge(lo_ready, number(n0 + 1, e))
                for tt, b in enumerate(banks):
                    for kk in range(4):
                        last = three_passes(bank(b), lhs(4 * half + kk, tt), panel(n0, 512 * kk, 512 * kk + 512),
                                            half == 0 and kk == 0, half == 1 and kk == 3)
                return last.then_inc(panel_used, 1)

            def tall_panel(n0, e, banks, lhs, start, stop):
                pe.wait_ge(lo_ready, number(n0 + 1, e))
                for tt, pair in enumerate(banks):
                    for kk in range(2):
                        for k, b in enumerate(pair):
                            at = D * kk + 512 * k
                            last = three_passes(bank(b), lhs(kk, tt), panel(n0, at, at + 512),
                                                start and kk == 0, stop and kk == 1)
                return last.then_inc(panel_used, 1)

            def x_cols(kt, tt):
                at = (slice(None), kt, slice(tt * P, tt * P + P))
                return xT_hi[at], xT_lo[at]

            def transpose_x(r):
                for b in range(4):
                    if r:
                        pe.wait_ge(x_ready, 4 * (r - 1) + (2 if b < 2 else 4))
                    for kt in (2 * b, 2 * b + 1):
                        for tt in range(TT):
                            at = (kt % 2) * T + tt * P
                            last = nc.tensor.transpose(bank(4 + b, at, at + P), X[:, tt, kt * P:kt * P + P], ident)
                    last.then_inc(xT_psum, 1)

            pe.wait_ge(x_in, 16)
            pe.wait_ge(consts_in, 16)
            transpose_x(0)
            pe.wait_ge(xT_lo_ready, 4)
            for c in range(3):
                for half in range(2):
                    wide_panel(N_QKV + 2 * c + half, None, half, (2 * c, 2 * c + 1), x_cols)
            pe.wait_ge(v_ready, 2)
            pe.wait_ge(rope_added, 6)
            for b in range(QT // 2):
                for j in (2 * b, 2 * b + 1):
                    for tt in range(TT):
                        at = (j % 2) * T + tt * P
                        last = nc.tensor.transpose(bank(b, at, at + P), roped[:, tt, j, :], ident)
                last.then_inc(qkT_psum, 1)
            pe.wait_ge(qkT_act, 3)
            pe.wait_ge(qkT_dve, 2)

            for s in range(PAIRS + 2):
                if s < PAIRS:
                    if s >= 2:
                        pe.wait_ge(masked, s - 1)
                    for qb in range(TT):
                        for b in range(2):
                            rows = slice(HD * b, HD * b + HD)
                            last = nc.tensor.matmul(bank(2 * (s % 2) + b, qb * T, qb * T + T),
                                                    qkT[rows, s, qb * P:qb * P + P], qkT[rows, PAIRS + s // 4, :],
                                                    start=True, stop=True)
                    last.then_inc(scores, 1)
                if 1 <= s < PAIRS + 1:
                    j = s - 1
                    pe.wait_ge(probs_ready, j + 1)
                    if j:
                        pe.wait_ge(pT_act, j)
                        pe.wait_ge(pT_dve, j)
                    for b in range(2):
                        for kt in range(TT):
                            for qb in range(TT):
                                at = kt * T + qb * P
                                last = nc.tensor.transpose(bank(4 + b, at, at + P),
                                                           probs[:, j % 2, 2 * b + qb, kt * P:kt * P + P], ident)
                    last.then_inc(pT_psum, 1)
                if s >= 2:
                    j = s - 2
                    pe.wait_ge(pT_act, j + 1)
                    pe.wait_ge(pT_dve, j + 1)
                    if j >= 2:
                        pe.wait_ge(o_lo, j - 1)
                    for kt in range(TT):
                        for b in range(2):
                            kv = 2 * (j // 4) + b
                            last = nc.tensor.matmul(psum[HD * b:HD * b + HD, 6 + j % 2, 0:T],
                                                    v[:, kt, kv * HD:kv * HD + HD], pT[:, b, kt, :],
                                                    start=kt == 0, stop=kt == 1)
                    last.then_inc(o_psum, 1)
            pe.wait_ge(o_lo, PAIRS)
            pe.wait_ge(masked, PAIRS)
            for i in range(4):
                tall_panel(N_WO + i, None, ((0, 1), (2, 3)), lambda kk, tt: x_cols(2 * i + kk, tt), i == 0, i == 3)
            transpose_x(1)
            pe.wait_ge(xT_lo_ready, 8)

            def swiglu(first, e, nt, q0, lhs):
                gb, ub, yb = G_B[:nt], U_B[:nt], Y_B[:nt]

                def q(j):
                    return number_of(q0 + j, FB, e)

                def down(j, half):
                    if half == 0:
                        pe.wait_ge(hT_lo_ready, q(j) + 1)
                    def hidden(kk, tt):
                        return hT_hi[:, tt, 2 * half + kk, :], hT_lo[:, tt, 2 * half + kk, :]
                    tall_panel(first + FFN_AT["down", j, half], e, yb, hidden, j == 0 and half == 0,
                               j == FB - 1 and half == 1)

                for j in range(FB):
                    last_block = e is not None and j == FB - 1
                    if e is not None or j:
                        pe.wait_ge(silu_done, q(j))
                    for half in range(2):
                        wide_panel(first + FFN_AT["gate", j, half], e, half, gb, lhs)
                    if e is not None and j == 1:
                        pe.wait_ge(y_added, e * 4 + 5)
                        for st in range(TT):
                            for tt in range(TT):
                                last = nc.tensor.transpose(bank(4, st * T + tt * P, st * T + tt * P + P),
                                                           pick[:, tt, st * P:st * P + P].bitcast(fp32), ident)
                        last.then_inc(pickT_psum, 1)
                    if e is not None or j:
                        pe.wait_ge(hT_lo_ready, q(j))
                    for half in range(2):
                        wide_panel(first + FFN_AT["up", j, half], e, half, ub, lhs)
                    if e is not None and j == 1:
                        pe.wait_ge(pickT_ready, e + 2)
                    if j:
                        down(j - 1, 0)
                        if last_block:
                            pe.wait_ge(silu_done, q(j) + 1)
                            gather(e + 1, 0)
                        down(j - 1, 1)
                    if e is not None and j == 0:
                        pe.wait_ge(ye_lo_ready, e + 1)
                        pe.wait_ge(pickT_ready, e + 1)
                        scatter()
                    pe.wait_ge(h_ready, q(j) + 1)
                    for tt in range(nt):
                        for kk in range(4):
                            last = nc.tensor.transpose(bank(ub[tt], kk * P, kk * P + P), h[:, tt, kk * P:kk * P + P],
                                                       ident)
                    last.then_inc(hT_psum, 1)
                if e is not None:
                    gather(e + 1, 1)
                down(FB - 1, 0)
                if e is not None:
                    gather(e + 1, 2)
                down(FB - 1, 1)
                if e is not None:
                    gather(e + 1, 3)

            def gather(turn, i):
                if i:
                    pe.wait_ge(xg_hi_ready, turn * 4 + i)
                    pe.wait_ge(xg_lo_ready, turn * 4 + i)
                else:
                    pe.wait_ge(pick_ready, turn + 1)
                for b, part in enumerate((xT_hi, xT_lo)):
                    rows = part[:, :, :].rearrange("p k t -> p (k t)")
                    for kk in range(2):
                        for tt in range(TT):
                            at = tt * D + (2 * i + kk) * P
                            last = nc.tensor.matmul(bank(b, kk * T, kk * T + T), rows[:, at:at + P], pick[:, tt, :],
                                                    start=tt == 0, stop=tt == 1)
                last.then_inc(xg_psum, 1)

            def scatter():
                for tt in range(TT):
                    for k in range(2):
                        for st in range(TT):
                            for part in (ye_hi, ye_lo):
                                last = nc.tensor.matmul(bank(4 + 2 * tt + k), pickT[:, st, tt * P:tt * P + P],
                                                        part[:, st, 512 * k:512 * k + 512],
                                                        start=st == 0 and part is ye_hi, stop=st == 1 and part is ye_lo)
                last.then_inc(scattered, 1)

            swiglu(N_FFN, None, TT, 0, x_cols)

            pe.wait_ge(conv_in, 96)
            pe.wait_ge(pads_zero, 3)
            nc.tensor.transpose(bank(0, 0, 40), conv_rows[:, :], ident[0:40, 0:40])
            for m in range(KT):
                last = nc.tensor.transpose(bank(1, 32 * m, 32 * m + 32), tap_rows[:, m * P:m * P + P],
                                           ident[0:32, 0:32])
            last.then_inc(conv_colsT, 1)
            transpose_x(2)
            pe.wait_ge(xT_lo_ready, 12)
            pe.wait_ge(taps_ready, 2)
            for i in range(4):
                banks = range(0, 4) if i % 2 == 0 else range(4, 8)
                if i == 2:
                    pe.wait_ge(sig_done, 4)
                if i == 3:
                    pe.wait_ge(glu_done, 4)
                for half in range(2):
                    n0 = N_PW1 + 2 * i + half
                    pe.wait_ge(lo_ready, n0 + 1)
                    for m, b in enumerate(banks):
                        for kk in range(4):
                            at = 512 * kk + P * m
                            kt = 4 * half + kk
                            last = three_passes(bank(b, 0, T), panel(n0, at, at + P),
                                                (xT_hi[:, kt, :], xT_lo[:, kt, :]),
                                                half == 0 and kk == 0, half == 1 and kk == 3)
                    last.then_inc(panel_used, 1)
            pe.wait_ge(sig_done, 8)
            pe.wait_ge(glu_done, 8)
            for t, m in enumerate(PE_TILES):
                for i in range(TAP_GROUP):
                    pe.wait_ge(diag_ready, 32 * t + i + 1)
                    nc.tensor.matmul(bank(t, 0, T), diag[:, i, :], glu[:, m, i:i + T], start=i == 0,
                                     stop=False, skip_group_check=True).then_inc(diag_used, 1)
                with pe.Fori(1, 32 // TAP_GROUP) as group:
                    for i in range(TAP_GROUP):
                        pe.wait_ge(diag_ready, group * TAP_GROUP + (32 * t + i + 1))
                        last = nc.tensor.matmul(bank(t, 0, T), diag[:, i, :],
                                                glu[:, m, bass.ds(group * TAP_GROUP + i, T)], start=False,
                                                stop=False, skip_group_check=True)
                        last.then_inc(diag_used, 1)
            pe.wait_ge(conv_dve, TAPS * len(DVE_TILES))
            pe.wait_ge(conv_act, len(PE_TILES))
            for m in range(KT):
                last = nc.tensor.matmul(bank(4, 0, T), mean_w[:, :], cv[:, m, :], start=m == 0, stop=m == KT - 1)
            last.then_inc(mean_psum, 1)
            pe.wait_ge(squared, 1)
            for m in range(KT):
                last = nc.tensor.matmul(bank(5, 0, T), mean_w[:, :], cv_sq[:, m, :], start=m == 0, stop=m == KT - 1)
            last.then_inc(cvar_psum, 1)
            pe.wait_ge(z_lo, 2)
            for i in range(4):
                tall_panel(N_PW2 + i, None, ((0, 1), (2, 3)), lambda kk, tt: x_cols(2 * i + kk, tt), i == 0, i == 3)
            transpose_x(3)
            pe.wait_ge(xT_lo_ready, 16)

            pe.wait_ge(router_in, 16)
            for tt in range(TT):
                for kt in range(KT):
                    for part, s in enumerate(x_cols(kt, tt)):
                        last = nc.tensor.matmul(bank(tt, 0, EXPERTS), s.bitcast(fp32), router[:, kt, :],
                                                start=kt == 0 and part == 0, stop=kt == KT - 1 and part == 1)
            last.then_inc(logits_psum, 1)
            pe.wait_ge(chosen_ready, 1)
            nc.tensor.matmul(bank(2, 0, EXPERTS), tri, chosen[:, 0, :], start=True, stop=True)
            nc.tensor.matmul(bank(3, 0, EXPERTS), ones, chosen[:, 0, :], start=True, stop=False)
            nc.tensor.matmul(bank(3, 0, EXPERTS), tri, chosen[:, 1, :], start=False, stop=True)
            nc.tensor.matmul(bank(4, 0, EXPERTS), ones, chosen[:, 0, :], start=True, stop=False)
            nc.tensor.matmul(bank(4, 0, EXPERTS), ones, chosen[:, 1, :], start=False, stop=True).then_inc(slot_psum, 1)
            pe.wait_ge(routed, 1)

            def g_cols(kt, tt):
                at = (slice(None), kt, slice(tt * P, tt * P + P))
                return xg_hi[at], xg_lo[at]

            pe.wait_ge(x_hi_ready, 1)
            pe.wait_ge(x_lo_ready, 1)
            for i in range(4):
                gather(0, i)
            with pe.Fori(0, EXPERTS) as e:
                both_tiles = pe.value_load(two_tiles[0:1, bass.ds(e, 1)], min_val=0, max_val=1)
                pe.wait_ge(xg_hi_ready, e * 4 + 4)
                pe.wait_ge(xg_lo_ready, e * 4 + 4)
                with pe.If(both_tiles > 0):
                    swiglu(N_MOE, e, TT, FB, g_cols)
                with pe.Else():
                    swiglu(N_MOE, e, 1, FB, g_cols)
            pe.wait_ge(ye_lo_ready, EXPERTS + 1)
            pe.wait_ge(pickT_ready, EXPERTS + 1)
            scatter()


_INS = ['x', 'attn_w_qkv', 'attn_sink', 'attn_w_o', 'conv_pw1_w', 'conv_pw1_b', 'conv_dw_w', 'conv_dw_b',
        'conv_norm_g', 'conv_norm_b', 'conv_pw2_w', 'conv_pw2_b', 'ffn_w_gate', 'ffn_w_up', 'ffn_w_down',
        'moe_router', 'moe_w_gate', 'moe_w_up', 'moe_w_down', 'ln_mix_g', 'ln_mix_b', 'ln_ffn_g', 'ln_ffn_b']


def shape_constants():
    c = np.zeros((P, C_END), np.float32)
    r = np.arange(P)
    c[:, C_ID:C_ID + P] = np.eye(P)
    c[:, C_TRI:C_TRI + P] = r[:, None] < r[None, :]
    c[:, C_ONE:C_ONE + P] = 1.0
    c[:, C_IOTA:C_IOTA + 2 * P] = np.arange(2 * P)[None, :]
    keys = np.arange(T)
    for qb in range(TT):
        far = np.abs(keys[None, :] - (qb * P + r)[:, None]) > 128
        c[:, C_MASK + qb * T:C_MASK + qb * T + T] = np.where(far, np.float32(-1e30), np.float32(0))
    inv_freq = np.float32(10000.0) ** (-np.arange(0, HD, 2, dtype=np.float32) / np.float32(HD))
    for tt in range(TT):
        ang = (tt * P + r).astype(np.float32)[:, None] * inv_freq[None, :]
        c[:, C_COS + tt * 32:C_COS + tt * 32 + 32] = np.cos(ang)
        c[:, C_SIN + tt * 32:C_SIN + tt * 32 + 32] = np.sin(ang)
        c[:, C_NSIN + tt * 32:C_NSIN + tt * 32 + 32] = -np.sin(ang)
    return c


def kernel(**inputs):
    import concourse.bacc as bacc
    from concourse.bass_utils import run_bass_kernel_spmd

    nc = bacc.Bacc("TRN2", target_bir_lowering=False, num_devices=1)
    arrays, args = {}, []
    for name in _INS:
        a = np.ascontiguousarray(inputs[name])
        arrays[f"in_{name}_dram"] = a
        args.append(nc.dram_tensor(f"in_{name}_dram", a.shape, mybir.dt.from_np(a.dtype), kind="ExternalInput").ap())
    c = shape_constants()
    arrays["shape_consts_dram"] = c
    args.append(nc.dram_tensor("shape_consts_dram", c.shape, mybir.dt.float32, kind="ExternalInput").ap())
    args.append(nc.dram_tensor("out_0_dram", (1, T, D), mybir.dt.float32, kind="ExternalOutput").ap())
    build(nc, *args)
    r = run_bass_kernel_spmd(nc, [arrays], core_ids=[0])
    return r.results[0]["out_0_dram"]
```

```python
from contextlib import ExitStack

import concourse.bass as bass
from concourse import mybir
import numpy as np

P = 128
D = 1024
T = 256
TT = T // P
KT = D // P
HEADS, KV, HD = 16, 4, 64
PAIRS = HEADS // 2
QT = PAIRS + KV // 2
TAPS, HALF_TAPS = 31, 15
FF = 3584
FB = FF // 512
EXPERTS = 8
BANK = 512
PANEL = 2048
RAW, SPLIT = 7, 3
PER_FFN = 6 * FB
LN_EPS = 1e-5
ALPHA = 4.0 ** 0.25
DVE_EARLY, DVE_LATE, POOL_TILE, PE_TILES = (0, 1, 2), (4,), 3, (5, 6, 7)
TAP_GROUP = 4
EARLY_TAPS = 10

N_QKV = 0
N_WO = N_QKV + 6
N_FFN = N_WO + 4
N_PW1 = N_FFN + PER_FFN
N_PW2 = N_PW1 + 8
N_MOE = N_PW2 + 4

C_ID, C_TRI, C_ONE, C_IOTA = 0, 128, 256, 384
C_MASK = C_IOTA + 256
C_COS = C_MASK + 512
C_SIN = C_COS + TT * 32
C_NSIN = C_SIN + TT * 32
C_END = C_NSIN + TT * 32


def build(nc, x, attn_w_qkv, attn_sink, attn_w_o, conv_pw1_w, conv_pw1_b, conv_dw_w, conv_dw_b,
          conv_norm_g, conv_norm_b, conv_pw2_w, conv_pw2_b, ffn_w_gate, ffn_w_up, ffn_w_down,
          moe_router, moe_w_gate, moe_w_up, moe_w_down, ln_mix_g, ln_mix_b, ln_ffn_g, ln_ffn_b,
          shape_consts, out):
    fp32, f32r = mybir.dt.float32, mybir.dt.float32r
    u32, i32 = mybir.dt.uint32, mybir.dt.int32
    ALU, ACT, AX = mybir.AluOpType, mybir.ActivationFunctionType, mybir.AxisListType
    ctx = ExitStack()

    def sb(name, shape, dt=fp32, where=ctx):
        return where.enter_context(nc.sbuf_tensor(name, shape, dt))

    def sem(name):
        return ctx.enter_context(nc.semaphore(name))

    with ctx:
        raw = sb("raw", [P, RAW, PANEL])
        w_hi = sb("w_hi", [P, SPLIT, PANEL], f32r)
        w_lo = sb("w_lo", [P, SPLIT, PANEL], f32r)
        X = sb("X", [P, TT, D])
        xT_hi = sb("xT_hi", [P, KT, T], f32r)
        xT_lo = sb("xT_lo", [P, KT, T], f32r)
        consts = sb("consts", [P, C_END])
        ln_gb = sb("ln_gb", [P, 2, D])
        stats = sb("stats", [P, TT, 2, 6])
        mean_var = sb("mean_var", [P, TT, 2])
        var_eps = sb("var_eps", [P, TT])
        rstd = sb("rstd", [P, TT])
        minus_half = sb("minus_half", [P, TT])
        router = sb("router", [P, KT, EXPERTS])
        psum = ctx.enter_context(nc.psum_tensor("psum", [P, 8, BANK], fp32))
        ident = consts[:, C_ID:C_ID + P]
        ones = consts[:, C_ONE:C_ONE + P]
        tri = consts[:, C_TRI:C_TRI + P]

        attn = ExitStack()
        sink = sb("sink", [P, HEADS], where=attn)
        rope_cos = sb("rope_cos", [P, 2, BANK], where=attn)
        rope_sin = sb("rope_sin", [P, 2, BANK], where=attn)
        roped = sb("roped", [P, TT, QT, P], where=attn)
        qkT = sb("qkT", [P, QT, T], where=attn)
        v = sb("v", [P, TT, KV * HD], where=attn)
        neg_sink = sb("neg_sink", [P, HEADS], where=attn)
        probs = sb("probs", [P, 3, 4, T], where=attn)
        pT = sb("pT", [P, 2, 2, TT, T], where=attn)
        row_max = sb("row_max", [P, 3, 4], where=attn)
        neg_max = sb("neg_max", [P, 3, 4], where=attn)
        sink_arg = sb("sink_arg", [P, 3, 4], where=attn)
        sink_exp = sb("sink_exp", [P, 3, 4], where=attn)
        row_sum = sb("row_sum", [P, 3, 4], where=attn)
        denom = sb("denom", [P, 3, 4], where=attn)
        inv_denom = sb("inv_denom", [P, 3, 4], where=attn)
        attn.close()

        h_silu = sb("h_silu", [P, TT, BANK])
        h = sb("h", [P, TT, BANK])
        hT_hi = sb("hT_hi", [P, TT, 4, P], f32r)
        hT_lo = sb("hT_lo", [P, TT, 4, P], f32r)
        conv = ExitStack()
        conv_rows = sb("conv_rows", [40, P], where=conv)
        tap_rows = sb("tap_rows", [32, D], where=conv)
        conv_cols = sb("conv_cols", [P, 40], where=conv)
        taps = sb("taps", [P, KT, 32], where=conv)
        sig = sb("sig", [P, 4, T], where=conv)
        glu = sb("glu", [P, KT, T + 2 * HALF_TAPS + 2], where=conv)
        cv = sb("cv", [P, KT, T], where=conv)
        cv_sq = sb("cv_sq", [P, KT, T], where=conv)
        cv_var = sb("cv_var", [P, TT], where=conv)
        cv_rstd = sb("cv_rstd", [P, TT], where=conv)
        diag = sb("diag", [P, TAP_GROUP, P], where=conv)
        pool_term = sb("pool_term", [P, T], where=conv)
        late_sum = sb("late_sum", [P, T], where=conv)
        pw2_b = sb("pw2_b", [P, D], where=conv)
        mean_w = sb("mean_w", [P, P], where=conv)
        conv.close()

        xg_hi = sb("xg_hi", [P, KT, T], f32r)
        xg_lo = sb("xg_lo", [P, KT, T], f32r)
        ye_hi = sb("ye_hi", [P, TT, D], f32r)
        ye_lo = sb("ye_lo", [P, TT, D], f32r)
        y_acc = sb("y_acc", [P, TT, D])
        router_x = y_acc[:, :, :].rearrange("p t d -> p (t d)").rearrange("p (k t) -> p k t", k=KT)
        pick = sb("pick", [P, TT, T], f32r)
        pickT = sb("pickT", [P, TT, T], f32r)
        logitsT = sb("logitsT", [EXPERTS, T])
        logits = sb("logits", [P, TT, EXPERTS])
        top_val = sb("top_val", [P, TT, EXPERTS])
        top_idx = sb("top_idx", [P, TT, EXPERTS], u32)
        top_idx_f = sb("top_idx_f", [P, TT, EXPERTS])
        gate_arg = sb("gate_arg", [P, TT])
        gate_exp = sb("gate_exp", [P, TT])
        gates = sb("gates", [P, TT, 2])
        combine = sb("combine", [P, TT, EXPERTS + 1])
        combine2 = sb("combine2", [P, TT, EXPERTS])
        chosen = sb("chosen", [P, TT, EXPERTS])
        chosen2 = sb("chosen2", [P, TT, EXPERTS])
        slot = sb("slot", [P, TT, EXPERTS + 1])
        two_tiles = sb("two_tiles", [1, EXPERTS], i32)
        table_probe = sb("table_probe", [P, 1])

        landed = [sem(f"landed{i}") for i in range(RAW)]
        hi_ready = sem("hi_ready")
        lo_ready = sem("lo_ready")
        panel_used = sem("panel_used")
        x_in = [sem(f"x_in{half}") for half in range(2)]
        ident_in = sem("ident_in")
        consts_in = sem("consts_in")
        sink_in = sem("sink_in")
        gb_in = sem("gb_in")
        conv_in = sem("conv_in")
        router_in = sem("router_in")
        out_done = sem("out_done")
        dve_done = sem("dve_done")
        half_set = sem("half_set")
        x_ready = sem("x_ready")
        half_summed = sem("half_summed")
        var_ready = sem("var_ready")
        rstd_ready = sem("rstd_ready")
        xT_psum, xT_hi_ready, xT_lo_ready = sem("xT_psum"), sem("xT_hi_ready"), sem("xT_lo_ready")
        rope_terms, rope_added, v_ready = sem("rope_terms"), sem("rope_added"), sem("v_ready")
        qkT_psum, qkT_act, qkT_dve = sem("qkT_psum"), sem("qkT_act"), sem("qkT_dve")
        scores, masked, maxed, exped = sem("scores"), sem("masked"), sem("maxed"), sem("exped")
        probs_ready = sem("probs_ready")
        pT_psum, pT_act = sem("pT_psum"), sem("pT_act")
        o_psum, o_hi, o_lo = sem("o_psum"), sem("o_hi"), sem("o_lo")
        silu_done, h_ready = sem("silu_done"), sem("h_ready")
        hT_psum, hT_hi_ready, hT_lo_ready = sem("hT_psum"), sem("hT_hi_ready"), sem("hT_lo_ready")
        pads_zero, conv_colsT, taps_ready = sem("pads_zero"), sem("conv_colsT"), sem("taps_ready")
        sig_done, glu_done = sem("sig_done"), sem("glu_done")
        diag_ready, diag_used = sem("diag_ready"), sem("diag_used")
        conv_act, conv_dve, conv_pool = sem("conv_act"), sem("conv_dve"), sem("conv_pool")
        conv_late = sem("conv_late")
        pool_term_ready = sem("pool_term_ready")
        mean_psum, centred, squared, cvar_psum = sem("mean_psum"), sem("centred"), sem("squared"), sem("cvar_psum")
        cvar_ready, crstd_ready, scaled = sem("cvar_ready"), sem("crstd_ready"), sem("scaled")
        crstd_diag, crstd_psum = sem("crstd_diag"), sem("crstd_psum")
        act_out, z_hi, z_lo = sem("act_out"), sem("z_hi"), sem("z_lo")
        x_scaled = sem("x_scaled")
        logitsT_psum, logitsT_ready = sem("logitsT_psum"), sem("logitsT_ready")
        logits_psum, gate_arg_ready, gate_exp_ready = sem("logits_psum"), sem("gate_arg_ready"), sem("gate_exp_ready")
        chosen_ready, slot_psum, routed = sem("chosen_ready"), sem("slot_psum"), sem("routed")
        moe_zero = sem("moe_zero")
        rx_act, rx_dve = sem("rx_act"), sem("rx_dve")
        x_hi_ready, x_lo_ready, pick_ready = sem("x_hi_ready"), sem("x_lo_ready"), sem("pick_ready")
        xg_psum, xg_hi_ready, xg_lo_ready = sem("xg_psum"), sem("xg_hi_ready"), sem("xg_lo_ready")
        ye_hi_ready, ye_lo_ready = sem("ye_hi_ready"), sem("ye_lo_ready")
        pickT_psum, pickT_ready = sem("pickT_psum"), sem("pickT_ready")
        scattered, y_added = sem("scattered"), sem("y_added")

        assert PER_FFN % RAW == 0 and PER_FFN % SPLIT == 0
        dmas_before = [0] * (N_MOE + 1)
        seen = [0] * RAW
        for n in range(N_MOE):
            seen[n % RAW] += 2 if N_WO <= n < N_WO + 4 else 1
            dmas_before[n] = seen[n % RAW]

        def number_of(n0, per, e):
            return n0 if e is None else e * per + n0

        def number(n0, e):
            return number_of(n0, PER_FFN, e)

        def landed_at(n0, e):
            if n0 < N_MOE:
                return 16 * dmas_before[n0]
            return number_of(16 * (seen[n0 % RAW] + 1 + (n0 - N_MOE) // RAW), 16 * PER_FFN // RAW, e)

        def wide(w, half, c):
            return w[half * 512:half * 512 + 512, c * 512:c * 512 + 512].rearrange("(k p) n -> p k n", p=P)

        def tall(w, i):
            return w[i * 256:i * 256 + 256, :].rearrange("(k p) n -> p k n", p=P)

        def raw_as(n0, k):
            return raw[:, n0 % RAW, :].rearrange("p (k n) -> p k n", k=k)

        def ffn_panels():
            for j in range(FB):
                for kind in ("gate", "up"):
                    for half in range(2):
                        yield kind, j, half
                if j:
                    for half in range(2):
                        yield "down", j - 1, half
            for half in range(2):
                yield "down", FB - 1, half

        FFN_AT = {what: k for k, what in enumerate(ffn_panels())}

        G_B, U_B, Y_B = (0, 1), (2, 3), ((4, 5), (6, 7))

        XT_BANK = (4, 4, 0, 4)

        def gather_bank(turn, i):
            return 2 * i if isinstance(turn, int) else (0, 0, 2, 2)[i]

        def bank(i, a=0, b=BANK):
            return psum[:, i, a:b]

        def heads_view(ap):
            return ap.rearrange("p (h s d) -> p h s d", s=2, d=HD // 2)

        def rope_table(col, tt, n):
            t = consts[:, col + tt * 32:col + tt * 32 + 32]
            return t.unsqueeze(1).unsqueeze(1).broadcast_to([P, n, 2, 32]) if col == C_COS else \
                t.unsqueeze(1).broadcast_to([P, n, 32])

        block = ctx.enter_context(nc.Block())

        @block.sync
        def _(sp):
            def load(n0, e, dst_src):
                if n0 >= RAW:
                    sp.wait_ge(lo_ready, number(n0 - RAW + 1, e))
                for dst, src in dst_src:
                    sp.dma_start(dst, src).then_inc(landed[n0 % RAW], 16)

            def load_ffn(first, e, w_gate, w_up, w_down):
                for k, (kind, j, half) in enumerate(ffn_panels()):
                    if kind == "down":
                        src, dst = tall(w_down, 2 * j + half), raw_as(first + k, 2)
                    else:
                        src, dst = wide(w_gate if kind == "gate" else w_up, half, j), raw_as(first + k, 4)
                    load(first + k, e, [(dst, src)])

            sp.dma_start(ident, shape_consts[:, C_ID:C_ID + P]).then_inc(ident_in, 16)
            for half in range(2):
                cols = slice(512 * half, 512 * half + 512)
                sp.dma_start(X[:, :, cols], x[0].rearrange("(t p) d -> p t d", p=P)[:, :, cols]).then_inc(x_in[half], 16)
            for c in range(3):
                for half in range(2):
                    n = N_QKV + 2 * c + half
                    load(n, None, [(raw_as(n, 4), wide(attn_w_qkv[0], half, c))])
                if c == 0:
                    sp.dma_start(consts[:, P:], shape_consts[:, P:]).then_inc(consts_in, 16)
            wo = attn_w_o[0].rearrange("(kv g d) n -> kv d g n", kv=KV, d=HD)
            for i in range(4):
                n = N_WO + i
                load(n, None, [(raw_as(n, 2)[HD * b:HD * b + HD], wo[2 * (i // 2) + b][:, 2 * (i % 2):2 * (i % 2) + 2, :])
                               for b in range(2)])
            load_ffn(N_FFN, None, ffn_w_gate[0], ffn_w_up[0], ffn_w_down[0])
            for i, c in enumerate((2, 0, 3, 1)):
                for half in range(2):
                    n = N_PW1 + 2 * i + half
                    load(n, None, [(raw_as(n, 4), wide(conv_pw1_w[0], half, c))])
            for i in range(4):
                load(N_PW2 + i, None, [(raw_as(N_PW2 + i, 2), tall(conv_pw2_w[0], i))])

            with sp.Fori(0, EXPERTS) as e:
                load_ffn(N_MOE, e, moe_w_gate[0, bass.ds(e, 1)][0], moe_w_up[0, bass.ds(e, 1)][0],
                         moe_w_down[0, bass.ds(e, 1)][0])
            for k in range(2):
                load(N_MOE + k, EXPERTS, [(raw_as(N_MOE + k, 4), wide(moe_w_gate[0, 0], k, 0))])
            for tt in range(TT):
                sp.wait_ge(x_ready, 12 + 2 * tt + 2)
                sp.dma_start(out[0, tt * P:tt * P + P, :], X[:, tt, :]).then_inc(out_done, 16)
            sp.wait_ge(out_done, 32)

        @block.gpsimd
        def _(pool):
            pool.dma_start(sink[:, :], attn_sink[0].partition_broadcast(P)).then_inc(sink_in, 16)

            def load_norm(i, g, b):
                if i:
                    pool.wait_ge(x_ready, 4 * i)
                pool.dma_start(ln_gb[:, 0, :], g.partition_broadcast(P)).then_inc(gb_in, 16)
                pool.dma_start(ln_gb[:, 1, :], b.partition_broadcast(P)).then_inc(gb_in, 16)

            load_norm(0, ln_mix_g[0], ln_mix_b[0])
            nc.gpsimd.memset(minus_half[:, :], -0.5).then_inc(half_set, 1)

            for c in range(3):
                for tt in range(TT):
                    i = 2 * c + tt
                    pool.wait_ge(rope_terms, i + 1)
                    n = 4 if c == 2 else 8
                    a, b = rope_cos[:, i % 2, 0:n * HD], rope_sin[:, i % 2, 0:n * HD]
                    if c == 2:
                        o = roped[:, tt, PAIRS:QT, :].rearrange("p a n -> p (a n)")
                    else:
                        a = a.rearrange("p (b g d) -> p b g d", b=2, d=HD)
                        b = b.rearrange("p (b g d) -> p b g d", b=2, d=HD)
                        o = roped[:, tt, 4 * c:4 * c + 4, :].rearrange("p g (b d) -> p b g d", b=2)
                    nc.gpsimd.tensor_tensor(o, a, b, ALU.add).then_inc(rope_added, 1)

            def root(i):
                pool.wait_ge(half_set, 1)
                for tt in range(TT):
                    pool.wait_ge(var_ready, 2 * i + tt + 1)
                    nc.gpsimd.tensor_tensor(rstd[:, tt:tt + 1], var_eps[:, tt:tt + 1],
                                            minus_half[:, tt:tt + 1], ALU.pow).then_inc(rstd_ready, 1)

            root(0)
            load_norm(1, ln_ffn_g[0], ln_ffn_b[0])
            nc.gpsimd.memset(glu[:, :, :], 0.0).then_inc(pads_zero, 1)
            nc.gpsimd.memset(tap_rows[:, :], 0.0).then_inc(pads_zero, 1)
            nc.gpsimd.memset(mean_w[:, :], 1.0 / D).then_inc(pads_zero, 1)
            pool.wait_ge(pads_zero, 2)
            pool.dma_start(tap_rows[0:TAPS, :], conv_dw_w[0]).then_inc(conv_in, 16)
            for at, vec in ((0, conv_pw1_b), (16, conv_dw_b), (24, conv_norm_g), (32, conv_norm_b)):
                rows = vec.shape[1] // P
                pool.dma_start(conv_rows[at:at + rows, :], vec[0].rearrange("(r c) -> r c", c=P)).then_inc(conv_in, 16)
            pool.dma_start(pw2_b[:, :], conv_pw2_b[0].partition_broadcast(P)).then_inc(conv_in, 16)
            pool.dma_start(router[:, :, :], moe_router[0].rearrange("(k p) e -> p k e", p=P)).then_inc(router_in, 16)
            root(1)
            load_norm(2, ln_mix_g[1], ln_mix_b[1])
            pool.wait_ge(xT_psum, 12)
            nc.gpsimd.tensor_scalar(X[:, :, :], X[:, :, :], ALPHA, None, ALU.mult).then_inc(x_scaled, 1)
            pool.wait_ge(x_scaled, 1)
            pool.wait_ge(conv_in, 96)
            for tt in range(TT):
                nc.gpsimd.tensor_tensor(X[:, tt, :], X[:, tt, :], pw2_b[:, :], ALU.add).then_inc(x_scaled, 1)
            m = POOL_TILE
            pool.wait_ge(taps_ready, 2)
            pool.wait_ge(glu_done, 4)
            nc.gpsimd.tensor_scalar(cv[:, m, :], glu[:, m, 0:T], taps[:, m, 0:1], conv_cols[:, 16 + m:17 + m],
                                    ALU.mult, ALU.add).then_inc(conv_pool, 1)
            with pool.Fori(1, TAPS) as tap:
                pool.wait_ge(conv_pool, tap)
                nc.gpsimd.tensor_tensor(pool_term[:, :], glu[:, m, bass.ds(tap, T)],
                                        taps[:, m, bass.ds(tap, 1)].broadcast_to([P, T]),
                                        ALU.mult).then_inc(pool_term_ready, 1)
                pool.wait_ge(pool_term_ready, tap)
                nc.gpsimd.tensor_tensor(cv[:, m, :], cv[:, m, :], pool_term[:, :], ALU.add).then_inc(conv_pool, 1)
            pool.wait_ge(cvar_ready, 1)
            nc.gpsimd.tensor_tensor(cv_rstd[:, :], cv_var[:, :], minus_half[:, :], ALU.pow).then_inc(crstd_ready, 1)
            root(2)
            load_norm(3, ln_ffn_g[1], ln_ffn_b[1])
            nc.gpsimd.memset(ye_hi[:, :, :].bitcast(fp32), 0.0).then_inc(ye_hi_ready, 1)
            nc.gpsimd.memset(ye_lo[:, :, :].bitcast(fp32), 0.0).then_inc(ye_lo_ready, 1)
            nc.gpsimd.memset(pickT[:, :, :].bitcast(fp32), 0.0).then_inc(pickT_ready, 1)
            nc.gpsimd.memset(slot[:, :, :], -1.0).then_inc(moe_zero, 1)
            nc.gpsimd.memset(table_probe[:, :], 0.0).then_inc(moe_zero, 1)
            nc.gpsimd.memset(combine[:, :, :], 0.0).then_inc(moe_zero, 1)
            pool.wait_ge(logits_psum, 1)
            nc.gpsimd.tensor_scalar(y_acc[:, :, :], X[:, :, :], ALPHA, None, ALU.mult).then_inc(y_added, 1)
            root(3)

        @block.scalar
        def _(act):
            def round_panel(n0, e=None):
                act.wait_ge(landed[n0 % RAW], landed_at(n0, e))
                if n0 >= SPLIT:
                    act.wait_ge(panel_used, number(n0 - SPLIT + 1, e))
                nc.scalar.activation(w_hi[:, n0 % SPLIT, :], raw[:, n0 % RAW, :], ACT.Copy).then_inc(hi_ready, 1)

            def round_xT(r):
                for b in range(4):
                    act.wait_ge(xT_psum, 4 * r + b + 1)
                    nc.scalar.activation(xT_hi[:, 2 * b:2 * b + 2, :].rearrange("p k t -> p (k t)"),
                                         bank(XT_BANK[r] + b),
                                         ACT.Copy).then_inc(xT_hi_ready, 1)

            round_xT(0)
            for n in range(6):
                round_panel(n)
            for tt in range(TT):
                act.wait_ge(rope_terms, 5 + tt)
                nc.scalar.activation(v[:, tt, :], bank(4 + tt, 256), ACT.Copy).then_inc(v_ready, 1)
            round_panel(N_WO)
            for b in (0, 2, 4):
                act.wait_ge(qkT_psum, b + 1)
                nc.scalar.activation(qkT[:, 2 * b:2 * b + 2, :].rearrange("p k t -> p (k t)"), bank(b),
                                     ACT.Copy).then_inc(qkT_act, 1)
            round_panel(N_WO + 1)
            round_panel(N_WO + 2)

            for s in range(PAIRS + 2):
                if s < PAIRS:
                    k = s % 3
                    act.wait_ge(maxed, s + 1)
                    if s >= 3:
                        act.wait_ge(probs_ready, s - 2)
                    for i in range(4):
                        nc.scalar.activation(probs[:, k, i, :], probs[:, k, i, :], ACT.Exp,
                                             bias=neg_max[:, k, i:i + 1], accum_out=row_sum[:, k, i:i + 1])
                    nc.scalar.activation(sink_exp[:, k, :], sink_arg[:, k, :], ACT.Exp).then_inc(exped, 1)
                if 1 <= s < PAIRS + 1:
                    j = s - 1
                    act.wait_ge(pT_psum, j + 1)
                    if j >= 2:
                        act.wait_ge(o_psum, j - 1)
                    nc.scalar.activation(pT[:, j % 2, :, :, :].rearrange("p b k t -> p b (k t)"), psum[:, 4:6, :],
                                         ACT.Copy).then_inc(pT_act, 1)
                if s >= 2:
                    j = s - 2
                    act.wait_ge(o_psum, j + 1)
                    nc.scalar.activation(xT_hi[:, j, :], bank(6 + j % 2, 0, T), ACT.Copy).then_inc(o_hi, 1)

            round_panel(N_WO + 3)
            round_panel(N_FFN)
            round_xT(1)

            def swiglu(first, e, nt, q0):
                def q(j):
                    return number_of(q0 + j, FB, e)

                def panel(kind, j, half):
                    if e is None and kind == "gate" and j == 0 and half == 0:
                        return
                    round_panel(first + FFN_AT[kind, j, half], e)

                def round_hT(j):
                    act.wait_ge(hT_psum, q(j) + 1)
                    nc.scalar.activation(hT_hi[:, 0:nt].rearrange("p t k n -> p t (k n)"), psum[:, 2:2 + nt, :],
                                         ACT.Copy).then_inc(hT_hi_ready, 1)

                if e is not None:
                    nc.scalar.activation(table_probe[:, :], table_probe[:, :], ACT.Silu)
                for j in range(FB):
                    if j or e is None:
                        panel("gate", j, 0)
                        panel("gate", j, 1)
                    if j:
                        round_hT(j - 1)
                    panel("up", j, 0)
                    panel("up", j, 1)
                    act.wait_ge(panel_used, number(first + FFN_AT["gate", j, 1] + 1, e))
                    if e is not None or j:
                        act.wait_ge(h_ready, q(j))
                    nc.scalar.activation(h_silu[:, 0:nt, :], psum[:, 0:nt, :], ACT.Silu).then_inc(silu_done, 1)
                    if e is not None and j == 1:
                        act.wait_ge(pickT_psum, e + 1)
                        nc.scalar.activation(pickT[:, :, :].rearrange("p s t -> p (s t)"), bank(4),
                                             ACT.Copy).then_inc(pickT_ready, 1)
                    if j:
                        panel("down", j - 1, 0)
                        panel("down", j - 1, 1)
                if e is not None:
                    copy_gathered(e + 1, 0)
                panel("down", FB - 1, 0)
                round_hT(FB - 1)
                if e is not None:
                    copy_gathered(e + 1, 1)
                panel("down", FB - 1, 1)
                if e is not None:
                    round_panel(first + PER_FFN, e)
                    copy_gathered(e + 1, 2)
                    round_panel(first + PER_FFN + 1, e)
                    copy_gathered(e + 1, 3)
                    act.wait_ge(panel_used, number(first + PER_FFN, e))
                    nc.scalar.activation(ye_hi[:, 0:nt, :].rearrange("p s (k n) -> p (s k) n", k=2),
                                         psum[:, 4:4 + 2 * nt, :], ACT.Copy).then_inc(ye_hi_ready, 1)

            def copy_gathered(turn, i):
                act.wait_ge(xg_psum, turn * 4 + (i + 1))
                nc.scalar.activation(xg_hi[:, 2 * i:2 * i + 2, :].rearrange("p k t -> p (k t)"),
                                     bank(gather_bank(turn, i)),
                                     ACT.Copy).then_inc(xg_hi_ready, 1)

            swiglu(N_FFN, None, TT, 0)
            round_panel(N_PW1)
            act.wait_ge(conv_colsT, 1)
            nc.scalar.activation(conv_cols[:, :], bank(0, 0, 40), ACT.Copy).then_inc(taps_ready, 1)
            nc.scalar.activation(taps[:, :, :].rearrange("p k t -> p (k t)"), bank(1, 0, KT * 32),
                                 ACT.Copy).then_inc(taps_ready, 1)
            round_panel(N_PW1 + 1)
            round_xT(2)
            act.wait_ge(taps_ready, 2)
            for n in range(N_PW1 + 2, N_PW1 + 8):
                round_panel(n)
                if n in (N_PW1 + 2, N_PW1 + 6):
                    c = (n - N_PW1) // 4
                    act.wait_ge(panel_used, n)
                    if c:
                        act.wait_ge(glu_done, 4)
                    for m in range(4):
                        col = 8 + 4 * c + m
                        nc.scalar.activation(sig[:, m, :], bank(4 + m, 0, T), ACT.Sigmoid,
                                             bias=conv_cols[:, col:col + 1]).then_inc(sig_done, 1)
            for t, m in enumerate(PE_TILES):
                def diagonal(i, tap, group):
                    if t or group is not None:
                        before = (32 * t if group is None else group * TAP_GROUP + 32 * t) + i + 1 - TAP_GROUP
                        act.wait_ge(diag_used, before)
                    nc.scalar.activation(diag[:, i, :], ident, ACT.Copy, scale=tap).then_inc(diag_ready, 1)

                for i in range(TAP_GROUP):
                    diagonal(i, taps[:, m, i:i + 1], None)
                with act.Fori(1, 32 // TAP_GROUP) as group:
                    for i in range(TAP_GROUP):
                        diagonal(i, taps[:, m, bass.ds(group * TAP_GROUP + i, 1)], group)
                if t < 2:
                    round_panel(N_PW2 + t)
            for t, m in enumerate(PE_TILES):
                act.wait_ge(diag_used, 32 * (t + 1))
                nc.scalar.activation(cv[:, m, :], bank(5 + t, 0, T), ACT.Identity,
                                     bias=conv_cols[:, 16 + m:17 + m]).then_inc(conv_act, 1)
            for i in range(4):
                act.wait_ge(centred, i + 1)
                nc.scalar.activation(cv_sq[:, 2 * i:2 * i + 2, :], cv[:, 2 * i:2 * i + 2, :],
                                     ACT.Square).then_inc(squared, 1)
            round_panel(N_PW2 + 2)
            for i in range(4):
                act.wait_ge(scaled, i + 1)
                for m in (2 * i, 2 * i + 1):
                    nc.scalar.activation(cv_sq[:, m, :], cv[:, m, :], ACT.Silu, scale=conv_cols[:, 24 + m:25 + m],
                                         bias=conv_cols[:, 32 + m:33 + m]).then_inc(act_out, 1)
                act.wait_ge(act_out, 2 * i + 2)
                nc.scalar.activation(xT_hi[:, 2 * i:2 * i + 2, :], cv_sq[:, 2 * i:2 * i + 2, :], ACT.Copy).then_inc(z_hi, 1)
            round_panel(N_PW2 + 3)
            round_panel(N_MOE)
            round_panel(N_MOE + 1)
            for b in (0, 2):
                act.wait_ge(xT_psum, 12 + b + 1)
                nc.scalar.activation(router_x[:, 2 * b:2 * b + 2, :].rearrange("p k t -> p (k t)"), bank(4 + b),
                                     ACT.Copy).then_inc(rx_act, 1)
            act.wait_ge(x_ready, 12)
            nc.scalar.activation(xT_hi[:, :, :].rearrange("p k t -> p (k t)"), X[:, :, :].rearrange("p t d -> p (t d)"),
                                 ACT.Copy).then_inc(x_hi_ready, 1)
            act.wait_ge(gate_arg_ready, 1)
            nc.scalar.activation(gate_exp[:, :], gate_arg[:, :], ACT.Exp).then_inc(gate_exp_ready, 1)
            act.wait_ge(moe_zero, 3)
            for i in range(4):
                copy_gathered(0, i)
            act.wait_ge(routed, 1)
            with act.Fori(0, EXPERTS) as e:
                both_tiles = act.value_load(two_tiles[0:1, bass.ds(e, 1)], min_val=0, max_val=1)
                with act.If(both_tiles > 0):
                    swiglu(N_MOE, e, TT, FB)
                with act.Else():
                    swiglu(N_MOE, e, 1, FB)

        @block.vector
        def _(dve):
            steps = [0]

            def step(ins):
                steps[0] += 1
                ins.then_inc(dve_done, 1)
                dve.wait_ge(dve_done, steps[0])

            def rest_panel(n0, e=None):
                dve.wait_ge(hi_ready, number(n0 + 1, e))
                if n0 >= SPLIT:
                    dve.wait_ge(panel_used, number(n0 - SPLIT + 1, e))
                nc.vector.tensor_tensor(w_lo[:, n0 % SPLIT, :], raw[:, n0 % RAW, :],
                                        w_hi[:, n0 % SPLIT, :].bitcast(fp32), ALU.subtract).then_inc(lo_ready, 1)

            def rest_xT(r):
                for b in range(4):
                    dve.wait_ge(xT_hi_ready, 4 * r + b + 1)
                    d = slice(2 * b, 2 * b + 2)
                    nc.vector.tensor_tensor(xT_lo[:, d, :].rearrange("p k t -> p (k t)"), bank(XT_BANK[r] + b),
                                            xT_hi[:, d, :].rearrange("p k t -> p (k t)").bitcast(fp32),
                                            ALU.subtract).then_inc(xT_lo_ready, 1)

            rest_xT(0)
            for n in range(6):
                rest_panel(n)
            dve.wait_ge(consts_in, 16)
            for c in range(3):
                dve.wait_ge(panel_used, 2 * c + 2)
                for tt in range(TT):
                    i = 2 * c + tt
                    n = 4 if c == 2 else 8
                    src = heads_view(bank(2 * c + tt, 0, n * HD))
                    if i >= 2:
                        dve.wait_ge(rope_added, i - 1)
                    nc.vector.tensor_tensor(heads_view(rope_cos[:, i % 2, 0:n * HD]), src,
                                            rope_table(C_COS, tt, n), ALU.mult)
                    dst = heads_view(rope_sin[:, i % 2, 0:n * HD])
                    nc.vector.tensor_tensor(dst[:, :, 0, :], src[:, :, 1, :], rope_table(C_NSIN, tt, n), ALU.mult)
                    nc.vector.tensor_tensor(dst[:, :, 1, :], src[:, :, 0, :], rope_table(C_SIN, tt, n),
                                            ALU.mult).then_inc(rope_terms, 1)
            for b in (1, 3):
                dve.wait_ge(qkT_psum, b + 1)
                nc.vector.tensor_copy(qkT[:, 2 * b:2 * b + 2, :].rearrange("p k t -> p (k t)"),
                                      bank(b)).then_inc(qkT_dve, 1)
            dve.wait_ge(sink_in, 16)
            step(nc.vector.tensor_scalar(neg_sink[:, :], sink[:, :], -1.0, None, ALU.mult))
            mask = consts[:, C_MASK:C_MASK + 512].unsqueeze(1).broadcast_to([P, 2, 512])
            for s in range(PAIRS + 3):
                if s < PAIRS:
                    k = s % 3
                    dve.wait_ge(scores, s + 1)
                    if s >= 3:
                        dve.wait_ge(pT_psum, s - 2)
                    for b in range(2):
                        nc.vector.scalar_tensor_tensor(
                            probs[:, k, 2 * b:2 * b + 2, :].rearrange("p q t -> p (q t)"), bank(2 * (s % 2) + b),
                            HD ** -0.5, mask[:, 0, :], ALU.mult, ALU.add).then_inc(masked, 1)
                    for b in range(2):
                        dve.wait_ge(masked, 2 * s + b + 1)
                        last = nc.vector.reduce_max(row_max[:, k, 2 * b:2 * b + 2], probs[:, k, 2 * b:2 * b + 2, :], AX.X)
                    step(last)
                    first = (2 * (s // 4)) * 4 + s % 4
                    by_head = lambda t: t[:, k, :].rearrange("p (b q) -> p b q", b=2)
                    sinks = lambda t: t[:, first:first + 5:4].unsqueeze(2).broadcast_to([P, 2, 2])
                    step(nc.vector.scalar_tensor_tensor(by_head(neg_max), by_head(row_max), -1.0, sinks(neg_sink),
                                                        ALU.mult, ALU.min))
                    nc.vector.tensor_tensor(by_head(sink_arg), by_head(neg_max), sinks(sink), ALU.add).then_inc(maxed, 1)
                if 1 <= s < PAIRS + 1:
                    j = s - 1
                    k = j % 3
                    dve.wait_ge(exped, j + 1)
                    step(nc.vector.tensor_tensor(denom[:, k, :], row_sum[:, k, :], sink_exp[:, k, :], ALU.add))
                    step(nc.vector.reciprocal(inv_denom[:, k, :], denom[:, k, :]))
                    for i in range(4):
                        last = nc.vector.tensor_scalar(probs[:, k, i, :], probs[:, k, i, :],
                                                       inv_denom[:, k, i:i + 1], None, ALU.mult)
                    last.then_inc(probs_ready, 1)
                if s >= 3:
                    j = s - 3
                    dve.wait_ge(o_hi, j + 1)
                    nc.vector.tensor_tensor(xT_lo[:, j, :], bank(6 + j % 2, 0, T), xT_hi[:, j, :].bitcast(fp32),
                                            ALU.subtract).then_inc(o_lo, 1)
                if s == PAIRS:
                    rest_panel(N_WO)
            for n in range(N_WO + 1, N_WO + 4):
                rest_panel(n)
            rest_panel(N_FFN)

            def layer_norm(i, mix, alpha, wait_half):
                halves = [slice(512 * k, 512 * k + 512) for k in range(2)]
                dve.wait_ge(gb_in, 32 * (i + 1))
                for tt in range(TT):
                    source = (lambda k: mix(tt, k)) if alpha is None else (lambda k: X[:, tt, halves[k]])
                    for k, s in enumerate(halves):
                        wait_half(tt, k)
                        if alpha is not None:
                            nc.vector.scalar_tensor_tensor(X[:, tt, s], X[:, tt, s], alpha, mix(tt, k),
                                                           ALU.mult, ALU.add).then_inc(dve_done, 1)
                            steps[0] += 1
                    for k, s in enumerate(halves):
                        if alpha is not None:
                            dve.wait_ge(dve_done, steps[0] - 1)
                        nc.vector.bn_stats(stats[:, tt, k, :], source(k)).then_inc(dve_done, 1)
                        steps[0] += 1
                    dve.wait_ge(dve_done, steps[0])
                    step(nc.vector.bn_aggr(mean_var[:, tt, :], stats[:, tt, :, :].rearrange("p k s -> p (k s)")))
                    nc.vector.tensor_scalar(var_eps[:, tt:tt + 1], mean_var[:, tt, 1:2], LN_EPS, None,
                                            ALU.add).then_inc(var_ready, 1)
                    for k, s in enumerate(halves):
                        nc.vector.scalar_tensor_tensor(X[:, tt, s], source(k), mean_var[:, tt, 0:1],
                                                       ln_gb[:, 0, s], ALU.subtract, ALU.mult).then_inc(dve_done, 1)
                        steps[0] += 1
                    dve.wait_ge(rstd_ready, 2 * i + tt + 1)
                    for k, s in enumerate(halves):
                        dve.wait_ge(dve_done, steps[0] - 1 + k)
                        nc.vector.scalar_tensor_tensor(X[:, tt, s], X[:, tt, s], rstd[:, tt:tt + 1],
                                                       ln_gb[:, 1, s], ALU.mult, ALU.add).then_inc(x_ready, 1)

            def summed(i, panels):
                return lambda tt, k: dve.wait_ge(panel_used, panels) if tt and k else \
                    dve.wait_ge(half_summed, 3 * i + 2 * tt + k + 1)

            layer_norm(0, lambda tt, k: bank(2 * tt + k), ALPHA, summed(0, N_WO + 4))
            rest_xT(1)

            def swiglu(first, e, nt, q0):
                def q(j):
                    return number_of(q0 + j, FB, e)

                def panel(kind, j, half):
                    if e is None and kind == "gate" and j == 0 and half == 0:
                        return
                    rest_panel(first + FFN_AT[kind, j, half], e)

                def rest_hT(j):
                    dve.wait_ge(hT_hi_ready, q(j) + 1)
                    flat = lambda t: t[:, 0:nt].rearrange("p t k n -> p t (k n)")
                    nc.vector.tensor_tensor(flat(hT_lo), psum[:, 2:2 + nt, :], flat(hT_hi).bitcast(fp32),
                                            ALU.subtract).then_inc(hT_lo_ready, 1)

                for j in range(FB):
                    if j or e is None:
                        panel("gate", j, 0)
                        panel("gate", j, 1)
                    if j:
                        rest_hT(j - 1)
                    if e is not None and j == 1:
                        add_scattered(e, 0)
                    panel("up", j, 0)
                    if e is not None and j == 1:
                        add_scattered(e, 1)
                    panel("up", j, 1)
                    if e is not None and j == 2:
                        dve.wait_ge(pickT_psum, e + 1)
                        one_hot(bass.ds(e + 1, 1))
                    if j:
                        panel("down", j - 1, 0)
                        panel("down", j - 1, 1)
                    dve.wait_ge(panel_used, number(first + FFN_AT["up", j, 1] + 1, e))
                    dve.wait_ge(silu_done, q(j) + 1)
                    if e is not None or j:
                        dve.wait_ge(hT_psum, q(j))
                    nc.vector.tensor_tensor(h[:, 0:nt, :], h_silu[:, 0:nt, :], psum[:, 2:2 + nt, :],
                                            ALU.mult).then_inc(h_ready, 1)
                if e is not None:
                    copy_gathered(e + 1, 0)
                panel("down", FB - 1, 0)
                rest_hT(FB - 1)
                if e is not None:
                    copy_gathered(e + 1, 1)
                panel("down", FB - 1, 1)
                if e is not None:
                    rest_panel(first + PER_FFN, e)
                    copy_gathered(e + 1, 2)
                    rest_panel(first + PER_FFN + 1, e)
                    copy_gathered(e + 1, 3)
                    dve.wait_ge(ye_hi_ready, e + 2)
                    rows = lambda t: t[:, 0:nt, :].rearrange("p s (k n) -> p (s k) n", k=2)
                    nc.vector.tensor_tensor(rows(ye_lo), psum[:, 4:4 + 2 * nt, :], rows(ye_hi).bitcast(fp32),
                                            ALU.subtract).then_inc(ye_lo_ready, 1)

            def copy_gathered(turn, i):
                dve.wait_ge(xg_psum, turn * 4 + (i + 1))
                nc.vector.tensor_copy(xg_lo[:, 2 * i:2 * i + 2, :].rearrange("p k t -> p (k t)"),
                                      bank(gather_bank(turn, i) + 1)).then_inc(xg_lo_ready, 1)

            def one_hot(e):
                for tt in range(TT):
                    last = nc.vector.tensor_scalar(pick[:, tt, :], consts[:, C_IOTA:C_IOTA + T], slot[:, tt, e], None,
                                                   ALU.is_equal)
                last.then_inc(pick_ready, 1)

            def add_scattered(e, tt):
                dve.wait_ge(scattered, e * 2 + (tt + 1))
                for k in range(2):
                    s = slice(512 * k, 512 * k + 512)
                    gate = combine[:, tt, e:e + 1] if e is EXPERTS else combine[:, tt, bass.ds(e, 1)]
                    dve.wait_ge(y_added, e * 4 + 1)
                    nc.vector.scalar_tensor_tensor(y_acc[:, tt, s], bank(4 + 2 * tt + k), gate, y_acc[:, tt, s],
                                                   ALU.mult, ALU.add).then_inc(y_added, 1)

            swiglu(N_FFN, None, TT, 0)
            rest_panel(N_PW1)
            layer_norm(1, lambda tt, k: bank(4 + 2 * tt + k), ALPHA, summed(1, N_FFN + PER_FFN))
            rest_xT(2)
            rest_panel(N_PW1 + 1)
            dve.wait_ge(taps_ready, 2)
            dve.wait_ge(pads_zero, 3)

            def gated(c):
                dve.wait_ge(panel_used, N_PW1 + 4 * c + 4)
                for m in range(4):
                    col = 4 * c + m
                    dve.wait_ge(sig_done, col + 1)
                    nc.vector.scalar_tensor_tensor(glu[:, col, HALF_TAPS:HALF_TAPS + T], bank(m, 0, T),
                                                   conv_cols[:, col:col + 1], sig[:, m, :], ALU.add,
                                                   ALU.mult).then_inc(glu_done, 1)

            def convolve(first_tap, taps_end):
                n = len(DVE_EARLY)
                if first_tap == 0:
                    for m in DVE_EARLY:
                        nc.vector.tensor_scalar(cv[:, m, :], glu[:, m, 0:T], taps[:, m, 0:1],
                                                conv_cols[:, 16 + m:17 + m], ALU.mult, ALU.add).then_inc(conv_dve, 1)
                with dve.Fori(max(first_tap, 1), taps_end) as tap:
                    for i, m in enumerate(DVE_EARLY):
                        dve.wait_ge(conv_dve, tap * n + (i + 1 - n))
                        nc.vector.scalar_tensor_tensor(cv[:, m, :], glu[:, m, bass.ds(tap, T)],
                                                       taps[:, m, bass.ds(tap, 1)], cv[:, m, :], ALU.mult,
                                                       ALU.add).then_inc(conv_dve, 1)

            for n in range(N_PW1 + 2, N_PW1 + 5):
                rest_panel(n)
            gated(0)
            rest_panel(N_PW1 + 5)
            rest_panel(N_PW1 + 6)
            dve.wait_ge(glu_done, 4)
            convolve(0, 4)
            rest_panel(N_PW1 + 7)
            convolve(4, EARLY_TAPS)
            gated(1)
            dve.wait_ge(glu_done, 8)
            (late,) = DVE_LATE
            n_early = len(DVE_EARLY)
            nc.vector.tensor_scalar(cv[:, late, :], glu[:, late, 0:T], taps[:, late, 0:1],
                                    conv_cols[:, 16 + late:17 + late], ALU.mult, ALU.add).then_inc(conv_late, 1)
            with dve.Fori(EARLY_TAPS, TAPS) as tap:
                for i, m in enumerate(DVE_EARLY):
                    dve.wait_ge(conv_dve, tap * n_early + (i + 1 - n_early))
                    nc.vector.scalar_tensor_tensor(cv[:, m, :], glu[:, m, bass.ds(tap, T)],
                                                   taps[:, m, bass.ds(tap, 1)], cv[:, m, :], ALU.mult,
                                                   ALU.add).then_inc(conv_dve, 1)
                dve.wait_ge(conv_late, tap - (EARLY_TAPS - 1))
                behind = tap - (EARLY_TAPS - 1)
                nc.vector.scalar_tensor_tensor(cv[:, late, :], glu[:, late, bass.ds(behind, T)],
                                               taps[:, late, bass.ds(behind, 1)], cv[:, late, :], ALU.mult,
                                               ALU.add).then_inc(conv_late, 1)
            done = TAPS - EARLY_TAPS + 1
            for tap in range(done, TAPS):
                own, first = (tap - done) % 2, tap - done == 1
                target = late_sum[:, :] if own else cv[:, late, :]
                if first:
                    ins = nc.vector.tensor_scalar(target, glu[:, late, tap:tap + T], taps[:, late, tap:tap + 1], None,
                                                  ALU.mult)
                else:
                    dve.wait_ge(conv_late, tap - 1 if tap > done else tap)
                    ins = nc.vector.scalar_tensor_tensor(target, glu[:, late, tap:tap + T], taps[:, late, tap:tap + 1],
                                                         target, ALU.mult, ALU.add)
                ins.then_inc(conv_late, 1)
            dve.wait_ge(conv_late, TAPS)
            nc.vector.tensor_tensor(cv[:, late, :], cv[:, late, :], late_sum[:, :], ALU.add).then_inc(conv_late, 1)
            by_token = lambda b, n: bank(b, 0, T).unsqueeze(1).broadcast_to([P, n, T])
            quarters = [slice(2 * i, 2 * i + 2) for i in range(4)]
            rest_panel(N_PW2)
            rest_panel(N_PW2 + 1)
            dve.wait_ge(mean_psum, 1)
            for m in quarters:
                nc.vector.tensor_tensor(cv[:, m, :], cv[:, m, :], by_token(4, 2), ALU.subtract).then_inc(centred, 1)
            dve.wait_ge(cvar_psum, 1)
            nc.vector.tensor_scalar(cv_var[:, :], psum[:, 5:8:2, 0], LN_EPS, None, ALU.add).then_inc(cvar_ready, 1)
            dve.wait_ge(crstd_ready, 1)
            for tt in range(TT):
                nc.vector.tensor_scalar(diag[:, tt, :], ident, cv_rstd[:, tt:tt + 1], None,
                                        ALU.mult).then_inc(crstd_diag, 1)
            dve.wait_ge(crstd_psum, 1)
            for m in quarters:
                nc.vector.tensor_tensor(cv[:, m, :], cv[:, m, :], by_token(6, 2), ALU.mult).then_inc(scaled, 1)
            for i, m in enumerate(quarters):
                dve.wait_ge(z_hi, i + 1)
                nc.vector.tensor_tensor(xT_lo[:, m, :], cv_sq[:, m, :], xT_hi[:, m, :].bitcast(fp32),
                                        ALU.subtract).then_inc(z_lo, 1)
            rest_panel(N_PW2 + 2)
            rest_panel(N_PW2 + 3)
            rest_panel(N_MOE)
            dve.wait_ge(x_scaled, 3)
            layer_norm(2, lambda tt, k: bank(2 * tt + k), 1.0, summed(2, N_PW2 + 4))
            for b in (1, 3):
                dve.wait_ge(xT_psum, 12 + b + 1)
                nc.vector.tensor_copy(router_x[:, 2 * b:2 * b + 2, :].rearrange("p k t -> p (k t)"),
                                      bank(4 + b)).then_inc(rx_dve, 1)
            dve.wait_ge(x_hi_ready, 1)
            nc.vector.tensor_tensor(xT_lo[:, :, :].rearrange("p k t -> p (k t)"),
                                    X[:, :, :].rearrange("p t d -> p (t d)"),
                                    xT_hi[:, :, :].rearrange("p k t -> p (k t)").bitcast(fp32),
                                    ALU.subtract).then_inc(x_lo_ready, 1)
            rest_panel(N_MOE + 1)

            dve.wait_ge(logitsT_psum, 1)
            nc.vector.tensor_copy(logitsT[:, :], psum[0:EXPERTS, 0, 0:T]).then_inc(logitsT_ready, 1)
            dve.wait_ge(logits_psum, 1)
            step(nc.vector.tensor_copy(logits[:, :, :].rearrange("p t e -> p (t e)"), bank(1, 0, TT * EXPERTS)))
            for tt in range(TT):
                last = nc.vector.max(top_val[:, tt, :], logits[:, tt, :])
            step(last)
            for tt in range(TT):
                last = nc.vector.max_index(top_idx[:, tt, :], top_val[:, tt, :], logits[:, tt, :])
            step(last)
            step(nc.vector.tensor_copy(top_idx_f[:, :, :], top_idx[:, :, :]))
            nc.vector.tensor_tensor(gate_arg[:, :], top_val[:, :, 1], top_val[:, :, 0],
                                    ALU.subtract).then_inc(gate_arg_ready, 1)
            iota8 = consts[:, C_IOTA:C_IOTA + EXPERTS]
            for tt in range(TT):
                last = nc.vector.tensor_scalar(chosen2[:, tt, :], iota8, top_idx_f[:, tt, 1:2], None, ALU.is_equal)
            step(last)
            for tt in range(TT):
                last = nc.vector.scalar_tensor_tensor(chosen[:, tt, :], iota8, top_idx_f[:, tt, 0:1],
                                                      chosen2[:, tt, :], ALU.is_equal, ALU.add)
            step(last)
            dve.wait_ge(moe_zero, 3)
            nc.vector.memset(combine[:, :, 0:1], 0.0).then_inc(chosen_ready, 1)
            dve.wait_ge(gate_exp_ready, 1)
            step(nc.vector.tensor_scalar(gate_arg[:, :], gate_exp[:, :], 1.0, None, ALU.add))
            step(nc.vector.reciprocal(gates[:, :, 0], gate_arg[:, :]))
            step(nc.vector.tensor_tensor(gates[:, :, 1], gates[:, :, 0], gate_exp[:, :], ALU.mult))
            for tt in range(TT):
                nc.vector.tensor_scalar(combine[:, tt, 1:], iota8, top_idx_f[:, tt, 0:1], gates[:, tt, 0:1],
                                        ALU.is_equal, ALU.mult)
                last = nc.vector.tensor_scalar(combine2[:, tt, :], iota8, top_idx_f[:, tt, 1:2], gates[:, tt, 1:2],
                                               ALU.is_equal, ALU.mult)
            step(last)
            step(nc.vector.tensor_tensor(combine[:, :, 1:], combine[:, :, 1:], combine2[:, :, :], ALU.add))
            dve.wait_ge(slot_psum, 1)
            for tt in range(TT):
                last = nc.vector.scalar_tensor_tensor(slot[:, tt, 0:EXPERTS], bank(2 + tt, 0, EXPERTS), 1.0,
                                                      chosen[:, tt, :], ALU.add, ALU.mult)
            step(last)
            step(nc.vector.tensor_scalar(slot[:, :, 0:EXPERTS], slot[:, :, 0:EXPERTS], -1.0, None, ALU.add))
            nc.vector.tensor_scalar(two_tiles[0:1, :], psum[0:1, 4, 0:EXPERTS], P + 0.5, None,
                                    ALU.is_gt).then_inc(routed, 1)
            one_hot(slice(0, 1))
            for i in range(4):
                copy_gathered(0, i)
            dve.wait_ge(routed, 1)
            with dve.Fori(0, EXPERTS) as e:
                both_tiles = dve.value_load(two_tiles[0:1, bass.ds(e, 1)], min_val=0, max_val=1)
                with dve.If(both_tiles > 0):
                    swiglu(N_MOE, e, TT, FB)
                with dve.Else():
                    swiglu(N_MOE, e, 1, FB)
            for tt in range(TT):
                add_scattered(EXPERTS, tt)
            layer_norm(3, lambda tt, k: y_acc[:, tt, 512 * k:512 * k + 512], None,
                       lambda tt, k: dve.wait_ge(y_added, 4 * EXPERTS + 2 * tt + k + 2))

        @block.tensor
        def _(pe):
            def three_passes(o, st, mv, start, stop):
                nc.tensor.matmul(o, st[0], mv[0], start=start, stop=False)
                nc.tensor.matmul(o, st[0], mv[1], start=False, stop=False)
                return nc.tensor.matmul(o, st[1], mv[0], start=False, stop=stop)

            def panel(n0, a, b):
                return w_hi[:, n0 % SPLIT, a:b], w_lo[:, n0 % SPLIT, a:b]

            def wide_panel(n0, e, half, banks, lhs):
                pe.wait_ge(lo_ready, number(n0 + 1, e))
                for tt, b in enumerate(banks):
                    for kk in range(4):
                        last = three_passes(bank(b), lhs(4 * half + kk, tt), panel(n0, 512 * kk, 512 * kk + 512),
                                            half == 0 and kk == 0, half == 1 and kk == 3)
                return last.then_inc(panel_used, 1)

            def tall_tile(n0, tt, pair, lhs, start, stop):
                last = []
                for k, b in enumerate(pair):
                    for kk in range(2):
                        at = D * kk + 512 * k
                        ins = three_passes(bank(b), lhs(kk, tt), panel(n0, at, at + 512),
                                           start and kk == 0, stop and kk == 1)
                    last.append(ins)
                return last

            def tall_panel(n0, e, banks, lhs, start, stop=False):
                pe.wait_ge(lo_ready, number(n0 + 1, e))
                for tt, pair in enumerate(banks):
                    last = tall_tile(n0, tt, pair, lhs, start, stop)
                return last[1].then_inc(panel_used, 1)

            def last_tall_panels(n0, banks, lhs0, lhs1):
                for tt, pair in enumerate(banks):
                    if tt == 0:
                        pe.wait_ge(lo_ready, n0 + 1)
                    first = tall_tile(n0, tt, pair, lhs0, False, False)
                    if tt == 0:
                        pe.wait_ge(lo_ready, n0 + 2)
                        for half in tall_tile(n0 + 1, tt, pair, lhs1, False, True):
                            half.then_inc(half_summed, 1)
                first[1].then_inc(panel_used, 1)
                half0, half1 = tall_tile(n0 + 1, tt, pair, lhs1, False, True)
                half0.then_inc(half_summed, 1)
                half1.then_inc(panel_used, 1)

            def x_cols(kt, tt):
                at = (slice(None), kt, slice(tt * P, tt * P + P))
                return xT_hi[at], xT_lo[at]

            def transpose_x(r):
                def put(kt, tt):
                    at = (kt % 2) * T + tt * P
                    return nc.tensor.transpose(bank(XT_BANK[r] + kt // 2, at, at + P), X[:, tt, kt * P:kt * P + P],
                                               ident)

                if r:
                    pe.wait_ge(x_ready, 4 * (r - 1) + 2)
                    for kt in range(KT):
                        put(kt, 0)
                for b in range(4):
                    if r:
                        pe.wait_ge(x_ready, 4 * (r - 1) + (3 if b < 2 else 4))
                    else:
                        pe.wait_ge(x_in[b // 2], 16)
                    for kt in (2 * b, 2 * b + 1):
                        if r == 0:
                            put(kt, 0)
                        last = put(kt, 1)
                    last.then_inc(xT_psum, 1)

            def wait_xT(r, half):
                pe.wait_ge(xT_lo_ready, 4 * r + 2 + 2 * half)

            pe.wait_ge(ident_in, 16)
            transpose_x(0)
            for c in range(3):
                for half in range(2):
                    wait_xT(0, half)
                    wide_panel(N_QKV + 2 * c + half, None, half, (2 * c, 2 * c + 1), x_cols)
            pe.wait_ge(v_ready, 2)
            pe.wait_ge(rope_added, 6)
            for b in range(QT // 2):
                for j in (2 * b, 2 * b + 1):
                    for tt in range(TT):
                        at = (j % 2) * T + tt * P
                        last = nc.tensor.transpose(bank(b, at, at + P), roped[:, tt, j, :], ident)
                last.then_inc(qkT_psum, 1)
            pe.wait_ge(qkT_act, 3)
            pe.wait_ge(qkT_dve, 2)

            for s in range(PAIRS + 3):
                if s < PAIRS:
                    if s >= 2:
                        pe.wait_ge(masked, 2 * (s - 1))
                    for b in range(2):
                        for qb in range(TT):
                            rows = slice(HD * b, HD * b + HD)
                            last = nc.tensor.matmul(bank(2 * (s % 2) + b, qb * T, qb * T + T),
                                                    qkT[rows, s, qb * P:qb * P + P], qkT[rows, PAIRS + s // 4, :],
                                                    start=True, stop=True)
                    last.then_inc(scores, 1)
                if 2 <= s < PAIRS + 2:
                    j = s - 2
                    pe.wait_ge(probs_ready, j + 1)
                    if j:
                        pe.wait_ge(pT_act, j)
                    for b in range(2):
                        for kt in range(TT):
                            for qb in range(TT):
                                at = kt * T + qb * P
                                last = nc.tensor.transpose(bank(4 + b, at, at + P),
                                                           probs[:, j % 3, 2 * b + qb, kt * P:kt * P + P], ident)
                    last.then_inc(pT_psum, 1)
                if s >= 3:
                    j = s - 3
                    pe.wait_ge(pT_act, j + 1)
                    if j >= 2:
                        pe.wait_ge(o_lo, j - 1)
                    for kt in range(TT):
                        for b in range(2):
                            kv = 2 * (j // 4) + b
                            last = nc.tensor.matmul(psum[HD * b:HD * b + HD, 6 + j % 2, 0:T],
                                                    v[:, kt, kv * HD:kv * HD + HD], pT[:, j % 2, b, kt, :],
                                                    start=kt == 0, stop=kt == 1)
                    last.then_inc(o_psum, 1)
            pe.wait_ge(o_lo, PAIRS)
            pe.wait_ge(masked, 2 * PAIRS)
            x_tiles = [lambda kk, tt, i=i: x_cols(2 * i + kk, tt) for i in range(4)]
            for i in range(2):
                tall_panel(N_WO + i, None, ((0, 1), (2, 3)), x_tiles[i], i == 0)
            last_tall_panels(N_WO + 2, ((0, 1), (2, 3)), x_tiles[2], x_tiles[3])
            transpose_x(1)

            def swiglu(first, e, nt, q0, lhs):
                gb, ub, yb = G_B[:nt], U_B[:nt], Y_B[:nt]

                def q(j):
                    return number_of(q0 + j, FB, e)

                def hidden(half):
                    return lambda kk, tt: (hT_hi[:, tt, 2 * half + kk, :], hT_lo[:, tt, 2 * half + kk, :])

                def down(j, half):
                    if half == 0:
                        pe.wait_ge(hT_lo_ready, q(j) + 1)
                    tall_panel(first + FFN_AT["down", j, half], e, yb, hidden(half), j == 0 and half == 0,
                               j == FB - 1 and half == 1)

                for j in range(FB):
                    last_block = e is not None and j == FB - 1
                    if e is not None or j:
                        pe.wait_ge(silu_done, q(j))
                    for half in range(2):
                        if e is None and j == 0:
                            wait_xT(1, half)
                        elif e is not None and j == 0:
                            pe.wait_ge(xg_hi_ready, e * 4 + (2 + 2 * half))
                            pe.wait_ge(xg_lo_ready, e * 4 + (2 + 2 * half))
                        wide_panel(first + FFN_AT["gate", j, half], e, half, gb, lhs)
                    if e is not None and j == 1:
                        pe.wait_ge(y_added, e * 4 + 3)
                        for st in range(TT):
                            for tt in range(TT):
                                last = nc.tensor.transpose(bank(4, st * T + tt * P, st * T + tt * P + P),
                                                           pick[:, tt, st * P:st * P + P].bitcast(fp32), ident)
                        last.then_inc(pickT_psum, 1)
                    if e is not None or j:
                        pe.wait_ge(hT_lo_ready, q(j))
                    for half in range(2):
                        wide_panel(first + FFN_AT["up", j, half], e, half, ub, lhs)
                    if e is not None and j == 1:
                        pe.wait_ge(pickT_ready, e + 2)
                        pe.wait_ge(y_added, e * 4 + 5)
                    if j:
                        down(j - 1, 0)
                        if last_block:
                            pe.wait_ge(silu_done, q(j) + 1)
                            gather(e + 1, 0)
                        down(j - 1, 1)
                    if e is not None and j == 0:
                        pe.wait_ge(ye_lo_ready, e + 1)
                        pe.wait_ge(pickT_ready, e + 1)
                        scatter()
                    pe.wait_ge(h_ready, q(j) + 1)
                    for tt in range(nt):
                        for kk in range(4):
                            last = nc.tensor.transpose(bank(ub[tt], kk * P, kk * P + P), h[:, tt, kk * P:kk * P + P],
                                                       ident)
                    last.then_inc(hT_psum, 1)
                if e is None:
                    pe.wait_ge(hT_lo_ready, FB)
                    last_tall_panels(first + PER_FFN - 2, yb, hidden(0), hidden(1))
                    return
                gather(e + 1, 1)
                down(FB - 1, 0)
                gather(e + 1, 2)
                down(FB - 1, 1)
                gather(e + 1, 3)

            def gather(turn, i):
                if isinstance(turn, int):
                    pe.wait_ge(pick_ready, 1)
                elif i:
                    pe.wait_ge(xg_hi_ready, turn * 4 + i)
                    pe.wait_ge(xg_lo_ready, turn * 4 + i)
                else:
                    pe.wait_ge(pick_ready, turn + 1)
                for b, part in enumerate((xT_hi, xT_lo)):
                    rows = part[:, :, :].rearrange("p k t -> p (k t)")
                    for kk in range(2):
                        for tt in range(TT):
                            at = tt * D + (2 * i + kk) * P
                            last = nc.tensor.matmul(bank(gather_bank(turn, i) + b, kk * T, kk * T + T),
                                                    rows[:, at:at + P], pick[:, tt, :],
                                                    start=tt == 0, stop=tt == 1)
                last.then_inc(xg_psum, 1)

            def scatter():
                for tt in range(TT):
                    for k in range(2):
                        for st in range(TT):
                            for part in (ye_hi, ye_lo):
                                last = nc.tensor.matmul(bank(4 + 2 * tt + k), pickT[:, st, tt * P:tt * P + P],
                                                        part[:, st, 512 * k:512 * k + 512],
                                                        start=st == 0 and part is ye_hi, stop=st == 1 and part is ye_lo)
                    last.then_inc(scattered, 1)

            swiglu(N_FFN, None, TT, 0, x_cols)

            pe.wait_ge(conv_in, 96)
            pe.wait_ge(pads_zero, 3)
            nc.tensor.transpose(bank(0, 0, 40), conv_rows[:, :], ident[0:40, 0:40])
            for m in range(KT):
                last = nc.tensor.transpose(bank(1, 32 * m, 32 * m + 32), tap_rows[:, m * P:m * P + P],
                                           ident[0:32, 0:32])
            last.then_inc(conv_colsT, 1)
            pe.wait_ge(taps_ready, 2)
            transpose_x(2)
            for i in range(4):
                banks = range(4, 8) if i % 2 == 0 else range(0, 4)
                if i == 2:
                    pe.wait_ge(sig_done, 4)
                if i == 3:
                    pe.wait_ge(glu_done, 4)
                for half in range(2):
                    wait_xT(2, half)
                    n0 = N_PW1 + 2 * i + half
                    pe.wait_ge(lo_ready, n0 + 1)
                    for m, b in enumerate(banks):
                        for kk in range(4):
                            at = 512 * kk + P * m
                            kt = 4 * half + kk
                            last = three_passes(bank(b, 0, T), panel(n0, at, at + P),
                                                (xT_hi[:, kt, :], xT_lo[:, kt, :]),
                                                half == 0 and kk == 0, half == 1 and kk == 3)
                    last.then_inc(panel_used, 1)
            pe.wait_ge(sig_done, 8)
            for t, m in enumerate(PE_TILES):
                pe.wait_ge(glu_done, m + 1)
                for i in range(TAP_GROUP):
                    pe.wait_ge(diag_ready, 32 * t + i + 1)
                    nc.tensor.matmul(bank(5 + t, 0, T), diag[:, i, :], glu[:, m, i:i + T], start=i == 0,
                                     stop=False, skip_group_check=True).then_inc(diag_used, 1)
                with pe.Fori(1, 32 // TAP_GROUP) as group:
                    for i in range(TAP_GROUP):
                        pe.wait_ge(diag_ready, group * TAP_GROUP + (32 * t + i + 1))
                        last = nc.tensor.matmul(bank(5 + t, 0, T), diag[:, i, :],
                                                glu[:, m, bass.ds(group * TAP_GROUP + i, T)], start=False,
                                                stop=False, skip_group_check=True)
                        last.then_inc(diag_used, 1)
            tiles = DVE_EARLY + (POOL_TILE,) + PE_TILES + DVE_LATE
            for k, m in enumerate(tiles):
                if m in PE_TILES:
                    pe.wait_ge(conv_act, PE_TILES.index(m) + 1)
                elif m == POOL_TILE:
                    pe.wait_ge(conv_pool, TAPS)
                elif m in DVE_EARLY:
                    pe.wait_ge(conv_dve, TAPS * len(DVE_EARLY))
                else:
                    pe.wait_ge(conv_late, TAPS + 1)
                last = nc.tensor.matmul(bank(4, 0, T), mean_w[:, :], cv[:, m, :], start=k == 0, stop=k == KT - 1)
            last.then_inc(mean_psum, 1)
            for i in range(4):
                pe.wait_ge(squared, i + 1)
                for tt in range(TT):
                    for m in (2 * i, 2 * i + 1):
                        last = nc.tensor.matmul(bank(5 + 2 * tt, 0, 1), cv_sq[:, m, tt * P:tt * P + P],
                                                mean_w[:, 0:1], start=m == 0, stop=m == KT - 1)
            last.then_inc(cvar_psum, 1)
            pe.wait_ge(crstd_diag, 2)
            for tt in range(TT):
                last = nc.tensor.matmul(bank(6, tt * P, tt * P + P), ones, diag[:, tt, :], start=True, stop=True)
            last.then_inc(crstd_psum, 1)
            for i in range(2):
                pe.wait_ge(z_lo, i + 1)
                tall_panel(N_PW2 + i, None, ((0, 1), (2, 3)), x_tiles[i], i == 0)
            pe.wait_ge(z_lo, 4)
            last_tall_panels(N_PW2 + 2, ((0, 1), (2, 3)), x_tiles[2], x_tiles[3])
            pe.wait_ge(scaled, 4)
            transpose_x(3)

            pe.wait_ge(router_in, 16)
            pe.wait_ge(rx_act, 2)
            pe.wait_ge(rx_dve, 2)
            for kt in range(KT):
                last = nc.tensor.matmul(psum[0:EXPERTS, 0, 0:T], router[:, kt, :], router_x[:, kt, :],
                                        start=kt == 0, stop=kt == KT - 1)
            last.then_inc(logitsT_psum, 1)
            pe.wait_ge(logitsT_ready, 1)
            for tt in range(TT):
                last = nc.tensor.transpose(bank(1, tt * EXPERTS, (tt + 1) * EXPERTS), logitsT[:, tt * P:tt * P + P],
                                           ident[0:EXPERTS, 0:EXPERTS])
            last.then_inc(logits_psum, 1)
            pe.wait_ge(chosen_ready, 1)
            nc.tensor.matmul(bank(2, 0, EXPERTS), tri, chosen[:, 0, :], start=True, stop=True)
            nc.tensor.matmul(bank(3, 0, EXPERTS), ones, chosen[:, 0, :], start=True, stop=False)
            nc.tensor.matmul(bank(3, 0, EXPERTS), tri, chosen[:, 1, :], start=False, stop=True)
            nc.tensor.matmul(bank(4, 0, EXPERTS), ones, chosen[:, 0, :], start=True, stop=False)
            nc.tensor.matmul(bank(4, 0, EXPERTS), ones, chosen[:, 1, :], start=False, stop=True).then_inc(slot_psum, 1)
            pe.wait_ge(routed, 1)

            def g_cols(kt, tt):
                at = (slice(None), kt, slice(tt * P, tt * P + P))
                return xg_hi[at], xg_lo[at]

            pe.wait_ge(x_hi_ready, 1)
            pe.wait_ge(x_lo_ready, 1)
            for i in range(4):
                gather(0, i)
            with pe.Fori(0, EXPERTS) as e:
                both_tiles = pe.value_load(two_tiles[0:1, bass.ds(e, 1)], min_val=0, max_val=1)
                with pe.If(both_tiles > 0):
                    swiglu(N_MOE, e, TT, FB, g_cols)
                with pe.Else():
                    swiglu(N_MOE, e, 1, FB, g_cols)
            pe.wait_ge(ye_lo_ready, EXPERTS + 1)
            pe.wait_ge(pickT_ready, EXPERTS + 1)
            scatter()


_INS = ['x', 'attn_w_qkv', 'attn_sink', 'attn_w_o', 'conv_pw1_w', 'conv_pw1_b', 'conv_dw_w', 'conv_dw_b',
        'conv_norm_g', 'conv_norm_b', 'conv_pw2_w', 'conv_pw2_b', 'ffn_w_gate', 'ffn_w_up', 'ffn_w_down',
        'moe_router', 'moe_w_gate', 'moe_w_up', 'moe_w_down', 'ln_mix_g', 'ln_mix_b', 'ln_ffn_g', 'ln_ffn_b']


def shape_constants():
    c = np.zeros((P, C_END), np.float32)
    r = np.arange(P)
    c[:, C_ID:C_ID + P] = np.eye(P)
    c[:, C_TRI:C_TRI + P] = r[:, None] < r[None, :]
    c[:, C_ONE:C_ONE + P] = 1.0
    c[:, C_IOTA:C_IOTA + 2 * P] = np.arange(2 * P)[None, :]
    keys = np.arange(T)
    for qb in range(TT):
        far = np.abs(keys[None, :] - (qb * P + r)[:, None]) > 128
        c[:, C_MASK + qb * T:C_MASK + qb * T + T] = np.where(far, np.float32(-1e30), np.float32(0))
    inv_freq = np.float32(10000.0) ** (-np.arange(0, HD, 2, dtype=np.float32) / np.float32(HD))
    for tt in range(TT):
        ang = (tt * P + r).astype(np.float32)[:, None] * inv_freq[None, :]
        c[:, C_COS + tt * 32:C_COS + tt * 32 + 32] = np.cos(ang)
        c[:, C_SIN + tt * 32:C_SIN + tt * 32 + 32] = np.sin(ang)
        c[:, C_NSIN + tt * 32:C_NSIN + tt * 32 + 32] = -np.sin(ang)
    return c


def kernel(**inputs):
    import concourse.bacc as bacc
    from concourse.bass_utils import run_bass_kernel_spmd

    nc = bacc.Bacc("TRN2", target_bir_lowering=False, num_devices=1)
    arrays, args = {}, []
    for name in _INS:
        a = np.ascontiguousarray(inputs[name])
        arrays[f"in_{name}_dram"] = a
        args.append(nc.dram_tensor(f"in_{name}_dram", a.shape, mybir.dt.from_np(a.dtype), kind="ExternalInput").ap())
    c = shape_constants()
    arrays["shape_consts_dram"] = c
    args.append(nc.dram_tensor("shape_consts_dram", c.shape, mybir.dt.float32, kind="ExternalInput").ap())
    args.append(nc.dram_tensor("out_0_dram", (1, T, D), mybir.dt.float32, kind="ExternalOutput").ap())
    build(nc, *args)
    r = run_bass_kernel_spmd(nc, [arrays], core_ids=[0])
    return r.results[0]["out_0_dram"]
```
